# Optimizing a Trainium2 kernel written in Bass

```python
import math
import jax
import jax.numpy as jnp
from jax import lax
import numpy as np
import jax, jax.numpy as jnp

D_MODEL = 1024
BATCH = 1
SEQ = 256
DEPTH = 2

N_A_LAYERS = DEPTH // 2
N_B_LAYERS = DEPTH - N_A_LAYERS

A_HEADS = 8
A_DK = 128
A_DV = 128
A_KEY_W = A_HEADS * A_DK
A_VAL_W = A_HEADS * A_DV
A_CONV_CH = 2 * A_KEY_W + A_VAL_W
A_IN_W = A_CONV_CH + A_VAL_W + 2 * A_HEADS
CONV_W = 4
CHUNK = 64

B_HEADS = 8
B_DH = 128
B_W = B_HEADS * B_DH
MOBA_BLOCK = 256
MOBA_TOPK = 3
Q_SUB = 32

N_BUCKETS = 32
MAX_DIST = 2048
EPS = 1e-6


def rms_norm(x, g):
    xf = x.astype(jnp.float32)
    y = xf * lax.rsqrt(jnp.mean(xf * xf, axis=-1, keepdims=True) + EPS)
    return (y * g.astype(jnp.float32)).astype(x.dtype)

def l2_normalize(t):
    tf = t.astype(jnp.float32)
    return tf * lax.rsqrt(jnp.sum(tf * tf, axis=-1, keepdims=True) + EPS)

def causal_conv_silu(u, w):
    c = u.shape[-1]
    up = jnp.pad(u, ((0, 0), (CONV_W - 1, 0), (0, 0)))
    out = lax.conv_general_dilated(up, w[:, None, :].astype(u.dtype), window_strides=(1,), padding="VALID", dimension_numbers=("NWC", "WIO", "NWC"), feature_group_count=c)
    return jax.nn.silu(out)

def gated_delta_rule(q, k, v, g, beta):
    bsz, s, h, dk = q.shape
    dv = v.shape[-1]
    n = s // CHUNK
    f32 = jnp.float32

    def to_chunks(t):
        t = t.astype(f32).reshape((bsz, n, CHUNK) + t.shape[2:])
        return jnp.moveaxis(t, 3, 1)

    q, k, v, g, beta = (to_chunks(t) for t in (q, k, v, g, beta))
    g = jnp.cumsum(g, axis=-1)
    idx = jnp.arange(CHUNK)
    tril = idx[:, None] >= idx[None, :]
    strict = idx[:, None] > idx[None, :]
    decay = jnp.exp(jnp.where(tril, g[..., :, None] - g[..., None, :], -jnp.inf))
    k_beta = k * beta[..., None]
    a_mat = jnp.where(strict, jnp.einsum("bhncd,bhnsd->bhncs", k_beta, k) * decay, 0.0)
    rhs = jnp.concatenate([v * beta[..., None], k_beta * jnp.exp(g)[..., None]], axis=-1)
    sol = lax.linalg.triangular_solve(a_mat + jnp.eye(CHUNK, dtype=f32), rhs, left_side=True, lower=True, unit_diagonal=True)
    u, w = sol[..., :dv], sol[..., dv:]
    qk_intra = jnp.where(tril, jnp.einsum("bhncd,bhnsd->bhncs", q, k) * decay, 0.0)
    q_dec = q * jnp.exp(g)[..., None]
    k_dec = k * jnp.exp(g[..., -1:] - g)[..., None]
    g_last = jnp.exp(g[..., -1])

    def step(state, xs):
        u_c, w_c, qd_c, qk_c, kd_c, gl_c = xs
        v_new = u_c - jnp.einsum("bhck,bhkv->bhcv", w_c, state)
        o = jnp.einsum("bhck,bhkv->bhcv", qd_c, state) + jnp.einsum("bhcs,bhsv->bhcv", qk_c, v_new)
        state = state * gl_c[..., None, None] + jnp.einsum("bhck,bhcv->bhkv", kd_c, v_new)
        return state, o

    xs = tuple(jnp.moveaxis(t, 2, 0) for t in (u, w, q_dec, qk_intra, k_dec, g_last))
    state0 = jnp.zeros((bsz, h, dk, dv), f32)
    _, o = lax.scan(step, state0, xs)
    return o.transpose(1, 0, 3, 2, 4).reshape(bsz, s, h, dv)

def gated_deltanet_mixer(hn, w_in, conv_w, a_log, dt_bias, out_norm_g, w_out):
    bsz, s, _ = hn.shape
    f32 = jnp.float32
    proj = hn @ w_in
    qkv = causal_conv_silu(proj[..., :A_CONV_CH], conv_w)
    z = proj[..., A_CONV_CH:A_CONV_CH + A_VAL_W]
    a = proj[..., A_CONV_CH + A_VAL_W:A_CONV_CH + A_VAL_W + A_HEADS]
    b = proj[..., A_CONV_CH + A_VAL_W + A_HEADS:]
    q = l2_normalize(qkv[..., :A_KEY_W].reshape(bsz, s, A_HEADS, A_DK)) * (A_DK ** -0.5)
    k = l2_normalize(qkv[..., A_KEY_W:2 * A_KEY_W].reshape(bsz, s, A_HEADS, A_DK))
    v = qkv[..., 2 * A_KEY_W:].reshape(bsz, s, A_HEADS, A_DV)
    g = -jnp.exp(a_log.astype(f32)) * jax.nn.softplus(a.astype(f32) + dt_bias.astype(f32))
    beta = jax.nn.sigmoid(b.astype(f32))
    o = gated_delta_rule(q, k, v, g, beta)
    o = rms_norm(o, out_norm_g) * jax.nn.silu(z.astype(f32)).reshape(bsz, s, A_HEADS, A_DV)
    return o.reshape(bsz, s, A_VAL_W).astype(hn.dtype) @ w_out

def t5_bucket(rel):
    n = jnp.maximum(rel, 0)
    max_exact = N_BUCKETS // 2
    nf = jnp.maximum(n, 1).astype(jnp.float32)
    large = max_exact + (jnp.log(nf / max_exact) / math.log(MAX_DIST / max_exact) * (N_BUCKETS - max_exact)).astype(jnp.int32)
    large = jnp.minimum(large, N_BUCKETS - 1)
    return jnp.where(n < max_exact, n, large)

def shared_kv(x, kv_norm_g, w_kv):
    bsz, s, _ = x.shape
    kv = rms_norm(x, kv_norm_g) @ w_kv
    n_blk = -(-s // MOBA_BLOCK)
    s_pad = n_blk * MOBA_BLOCK

    def blocks(t):
        t = jnp.pad(t.reshape(bsz, s, B_HEADS, B_DH), ((0, 0), (0, s_pad - s), (0, 0), (0, 0)))
        return t.reshape(bsz, n_blk, MOBA_BLOCK, B_HEADS, B_DH).transpose(0, 3, 1, 2, 4)

    kb = blocks(kv[..., :B_W])
    vb = blocks(kv[..., B_W:])
    k_mean = jnp.mean(kb.astype(jnp.float32), axis=3)
    return kb, vb, k_mean

def moba_attention(q, kb, vb, k_mean, rel_bias):
    bsz, s, h, d = q.shape
    n_blk = kb.shape[2]
    topk = min(MOBA_TOPK, n_blk)
    scale = d ** -0.5
    f32 = jnp.float32
    n_sub = s // Q_SUB
    q_sub = q.transpose(0, 2, 1, 3).reshape(bsz, h, n_sub, Q_SUB, d).transpose(2, 0, 1, 3, 4)
    bias_t = rel_bias.T.astype(f32)
    b_ix = jnp.arange(bsz)[:, None, None, None]
    h_ix = jnp.arange(h)[None, :, None, None]
    blk_ids = jnp.arange(n_blk)
    offs = jnp.arange(MOBA_BLOCK)

    def one_sub(args):
        qs, s_idx = args
        q_pos = s_idx * Q_SUB + jnp.arange(Q_SUB)
        cur = (s_idx * Q_SUB) // MOBA_BLOCK
        qf = qs.astype(f32)
        gate = jnp.einsum("bhqd,bhnd->bhqn", qf, k_mean)
        gate = jnp.where(blk_ids < cur, gate, -jnp.inf)
        _, sel = lax.top_k(gate, topk)
        sel_ok = jnp.arange(topk) < cur
        k_sel = kb[b_ix, h_ix, sel].astype(f32)
        v_sel = vb[b_ix, h_ix, sel].astype(f32)
        k_pos_sel = sel[..., None] * MOBA_BLOCK + offs
        s_sel = jnp.einsum("bhqd,bhqkjd->bhqkj", qf, k_sel) * scale
        s_sel = s_sel + bias_t[h_ix[..., None], t5_bucket(q_pos[:, None, None] - k_pos_sel)]
        s_sel = jnp.where(sel_ok[:, None], s_sel, -jnp.inf).reshape(bsz, h, Q_SUB, topk * MOBA_BLOCK)
        k_own = lax.dynamic_index_in_dim(kb, cur, axis=2, keepdims=False).astype(f32)
        v_own = lax.dynamic_index_in_dim(vb, cur, axis=2, keepdims=False).astype(f32)
        rel_own = q_pos[:, None] - (cur * MOBA_BLOCK + offs)[None, :]
        s_own = jnp.einsum("bhqd,bhjd->bhqj", qf, k_own) * scale + bias_t[:, t5_bucket(rel_own)]
        s_own = jnp.where(rel_own >= 0, s_own, -jnp.inf)
        p = jax.nn.softmax(jnp.concatenate([s_sel, s_own], axis=-1), axis=-1)
        p_sel = p[..., :topk * MOBA_BLOCK].reshape(bsz, h, Q_SUB, topk, MOBA_BLOCK)
        p_own = p[..., topk * MOBA_BLOCK:]
        o = jnp.einsum("bhqkj,bhqkjd->bhqd", p_sel, v_sel) + jnp.einsum("bhqj,bhjd->bhqd", p_own, v_own)
        return o.astype(qs.dtype)

    o = lax.map(one_sub, (q_sub, jnp.arange(n_sub)))
    return o.transpose(1, 0, 3, 2, 4).reshape(bsz, s, h * d)

def moba_mixer(hn, w_in, w_out, kb, vb, k_mean, rel_bias):
    bsz, s, _ = hn.shape
    proj = hn @ w_in
    q = proj[..., :B_W].reshape(bsz, s, B_HEADS, B_DH)
    z = proj[..., B_W:]
    o = moba_attention(q, kb, vb, k_mean, rel_bias)
    return (o * jax.nn.silu(z)).astype(hn.dtype) @ w_out

def first_inputs(seed: int = 0) -> dict:
    key = jax.random.key(seed)
    ks = jax.random.split(key, 16)
    f32 = jnp.float32
    na, nb = N_A_LAYERS, N_B_LAYERS

    def gain(k, shape):
        return 1.0 + 0.01 * jax.random.normal(k, shape, f32)

    x = jax.random.normal(ks[0], (BATCH, SEQ, D_MODEL), f32)
    a_norm_g = gain(ks[1], (na, D_MODEL))
    a_w_in = jax.random.normal(ks[2], (na, D_MODEL, A_IN_W), f32) * D_MODEL ** -0.5
    a_conv_w = jax.random.normal(ks[3], (na, CONV_W, A_CONV_CH), f32) * CONV_W ** -0.5
    a_log = jnp.log(jax.random.uniform(ks[4], (na, A_HEADS), f32, 1.0, 16.0))
    dt = jnp.exp(jax.random.uniform(ks[5], (na, A_HEADS), f32, math.log(1e-3), math.log(1e-1)))
    a_dt_bias = dt + jnp.log(-jnp.expm1(-dt))
    a_out_norm_g = gain(ks[6], (na, A_DV))
    a_w_out = jax.random.normal(ks[7], (na, A_VAL_W, D_MODEL), f32) * A_VAL_W ** -0.5
    kv_norm_g = gain(ks[8], (D_MODEL,))
    w_kv = jax.random.normal(ks[9], (D_MODEL, 2 * B_W), f32) * D_MODEL ** -0.5
    b_norm_g = gain(ks[10], (nb, D_MODEL))
    b_w_in = jax.random.normal(ks[11], (nb, D_MODEL, 2 * B_W), f32) * D_MODEL ** -0.5
    b_w_out = jax.random.normal(ks[12], (nb, B_W, D_MODEL), f32) * B_W ** -0.5
    rel_bias = 0.2 * jax.random.normal(ks[13], (N_BUCKETS, B_HEADS), f32)
    final_norm_g = gain(ks[14], (D_MODEL,))
    return {"x": x, "a_norm_g": a_norm_g, "a_w_in": a_w_in, "a_conv_w": a_conv_w, "a_log": a_log, "a_dt_bias": a_dt_bias, "a_out_norm_g": a_out_norm_g, "a_w_out": a_w_out, "kv_norm_g": kv_norm_g, "w_kv": w_kv, "b_norm_g": b_norm_g, "b_w_in": b_w_in, "b_w_out": b_w_out, "rel_bias": rel_bias, "final_norm_g": final_norm_g}

def first_block(x, a_norm_g, a_w_in, a_conv_w, a_log, a_dt_bias, a_out_norm_g, a_w_out, kv_norm_g, w_kv, b_norm_g, b_w_in, b_w_out, rel_bias, final_norm_g):
    shared = None
    for layer in range(DEPTH):
        if layer < N_A_LAYERS:
            i = layer
            x = x + gated_deltanet_mixer(rms_norm(x, a_norm_g[i]), a_w_in[i], a_conv_w[i], a_log[i], a_dt_bias[i], a_out_norm_g[i], a_w_out[i])
        else:
            if shared is None:
                shared = shared_kv(x, kv_norm_g, w_kv)
            j = layer - N_A_LAYERS
            kb, vb, k_mean = shared
            x = x + moba_mixer(rms_norm(x, b_norm_g[j]), b_w_in[j], b_w_out[j], kb, vb, k_mean, rel_bias)
    return rms_norm(x, final_norm_g)


BLOCK_Q = 128
NEG_INF = -1e30
ROPE_THETA = 10000.0

MLA_HEADS = 8
MLA_Q_RANK = 256
MLA_KV_RANK = 128
MLA_NOPE = 64
MLA_ROPE = 32
MLA_QK = MLA_NOPE + MLA_ROPE
MLA_V = 64
SB_HEADS = 8
SB_DIM = 64
SB_WIDTH = SB_HEADS * SB_DIM
FOX_HEADS = 16
FOX_DIM = 64
FOX_WIDTH = FOX_HEADS * FOX_DIM
D_FF = ((8 * D_MODEL // 3 + 255) // 256) * 256

EVEN_IN = MLA_Q_RANK + MLA_KV_RANK + MLA_ROPE + 3 * SB_WIDTH
EVEN_OUT = MLA_HEADS * MLA_V + SB_WIDTH
ODD_IN = 3 * FOX_WIDTH + FOX_HEADS
ODD_OUT = FOX_WIDTH


def rms_norm_2(x, g):
    xf = x.astype(jnp.float32)
    y = xf * lax.rsqrt(jnp.mean(xf * xf, axis=-1, keepdims=True) + EPS)
    return (y * g.astype(jnp.float32)).astype(x.dtype)

def split_last(x, sizes):
    return jnp.split(x, [int(v) for v in np.cumsum(sizes)[:-1]], axis=-1)

def heads_first(x):
    return x.transpose(0, 2, 1, 3)

def merge_heads(x):
    b, h, s, d = x.shape
    return x.transpose(0, 2, 1, 3).reshape(b, s, h * d)

def rope_tail(x, positions):
    nope, r = x[..., :-MLA_ROPE], x[..., -MLA_ROPE:]
    half = MLA_ROPE // 2
    inv_freq = ROPE_THETA ** (-jnp.arange(half, dtype=jnp.float32) / half)
    ang = positions.astype(jnp.float32)[..., None] * inv_freq
    cos, sin = jnp.cos(ang)[:, :, None, :], jnp.sin(ang)[:, :, None, :]
    r1, r2 = r[..., :half].astype(jnp.float32), r[..., half:].astype(jnp.float32)
    rot = jnp.concatenate([r1 * cos - r2 * sin, r2 * cos + r1 * sin], axis=-1)
    return jnp.concatenate([nope, rot.astype(x.dtype)], axis=-1)

def sweep_query_blocks(block_fn, q):
    b, h, s, _ = q.shape
    out = lax.map(block_fn, jnp.arange(s // BLOCK_Q))
    nb, _, _, bq, dv = out.shape
    return out.transpose(1, 2, 0, 3, 4).reshape(b, h, nb * bq, dv)

def causal_softmax_attention(q, k, v, scale, decay=None):
    s = k.shape[2]
    k_idx = jnp.arange(s)

    def block(i):
        start = i * BLOCK_Q
        qb = lax.dynamic_slice_in_dim(q, start, BLOCK_Q, axis=2)
        logits = jnp.einsum('bhqd,bhkd->bhqk', qb, k).astype(jnp.float32) * scale
        if decay is not None:
            cq = lax.dynamic_slice_in_dim(decay, start, BLOCK_Q, axis=2)
            logits = logits + cq[..., :, None] - decay[..., None, :]
        q_idx = start + jnp.arange(BLOCK_Q)
        mask = k_idx[None, :] <= q_idx[:, None]
        p = jax.nn.softmax(jnp.where(mask, logits, NEG_INF), axis=-1)
        return jnp.einsum('bhqk,bhkd->bhqd', p.astype(v.dtype), v)

    return sweep_query_blocks(block, q)

def stick_breaking_attention(q, k, v):
    s = k.shape[2]
    scale = q.shape[-1] ** -0.5
    k_idx = jnp.arange(s)

    def block(i):
        start = i * BLOCK_Q
        qb = lax.dynamic_slice_in_dim(q, start, BLOCK_Q, axis=2)
        z = jnp.einsum('bhqd,bhkd->bhqk', qb, k).astype(jnp.float32) * scale
        q_idx = start + jnp.arange(BLOCK_Q)
        mask = k_idx[None, :] < q_idx[:, None]
        log_beta = jax.nn.log_sigmoid(z)
        log_1m_beta = jnp.where(mask, jax.nn.log_sigmoid(-z), 0.0)
        suffix = lax.cumsum(log_1m_beta, axis=3, reverse=True) - log_1m_beta
        a = jnp.where(mask, jnp.exp(log_beta + suffix), 0.0)
        return jnp.einsum('bhqk,bhkd->bhqd', a.astype(v.dtype), v)

    return sweep_query_blocks(block, q)

def even_mixer(h, positions, w_in, q_a_norm, w_q_up, kv_a_norm, w_kv_up, q_norm, k_norm, w_o):
    b, s, _ = h.shape
    proj = h @ w_in
    cq, ckv, k_rope, sb_qkv = split_last(proj, [MLA_Q_RANK, MLA_KV_RANK, MLA_ROPE, 3 * SB_WIDTH])
    q = (rms_norm_2(cq, q_a_norm) @ w_q_up).reshape(b, s, MLA_HEADS, MLA_QK)
    kv = (rms_norm_2(ckv, kv_a_norm) @ w_kv_up).reshape(b, s, MLA_HEADS, MLA_NOPE + MLA_V)
    k_nope, v = kv[..., :MLA_NOPE], kv[..., MLA_NOPE:]
    k_rope = jnp.broadcast_to(k_rope[:, :, None, :], (b, s, MLA_HEADS, MLA_ROPE))
    k = jnp.concatenate([k_nope, k_rope], axis=-1)
    q = rope_tail(rms_norm_2(q, q_norm), positions)
    k = rope_tail(rms_norm_2(k, k_norm), positions)
    mla = causal_softmax_attention(heads_first(q), heads_first(k), heads_first(v), MLA_QK ** -0.5)
    sq, sk, sv = [heads_first(t.reshape(b, s, SB_HEADS, SB_DIM)) for t in jnp.split(sb_qkv, 3, axis=-1)]
    sb = stick_breaking_attention(sq, sk, sv)
    o = jnp.concatenate([merge_heads(mla), merge_heads(sb)], axis=-1)
    return o @ w_o

def odd_mixer(h, w_in, f_bias, q_norm, k_norm, w_o):
    b, s, _ = h.shape
    proj = h @ w_in
    q, k, v, f_logit = split_last(proj, [FOX_WIDTH, FOX_WIDTH, FOX_WIDTH, FOX_HEADS])
    q = rms_norm_2(q.reshape(b, s, FOX_HEADS, FOX_DIM), q_norm)
    k = rms_norm_2(k.reshape(b, s, FOX_HEADS, FOX_DIM), k_norm)
    v = v.reshape(b, s, FOX_HEADS, FOX_DIM)
    log_f = jax.nn.log_sigmoid(f_logit.astype(jnp.float32) + f_bias.astype(jnp.float32))
    decay = lax.cumsum(log_f, axis=1).transpose(0, 2, 1)
    o = causal_softmax_attention(heads_first(q), heads_first(k), heads_first(v), FOX_DIM ** -0.5, decay)
    return merge_heads(o) @ w_o

def swiglu(h, w_gate, w_up, w_down):
    return (jax.nn.silu(h @ w_gate) * (h @ w_up)) @ w_down

def second_inputs(seed: int = 0) -> dict:
    key = jax.random.key(seed)
    ks = iter(jax.random.split(key, 32))

    def dense(shape):
        return jax.random.normal(next(ks), shape, jnp.float32) * shape[0] ** -0.5

    def gain(n):
        return 1.0 + 0.1 * jax.random.normal(next(ks), (n,), jnp.float32)

    x = jax.random.normal(next(ks), (BATCH, SEQ, D_MODEL), jnp.float32)
    offsets = jax.random.randint(next(ks), (BATCH, 1), 0, SEQ, dtype=jnp.int32)
    positions = (offsets + jnp.arange(SEQ, dtype=jnp.int32)[None, :]).astype(jnp.int32)
    return {
        'x': x,
        'positions': positions,
        'l0_attn_norm': gain(D_MODEL),
        'l0_w_in': dense((D_MODEL, EVEN_IN)),
        'l0_mla_q_a_norm': gain(MLA_Q_RANK),
        'l0_mla_w_q_up': dense((MLA_Q_RANK, MLA_HEADS * MLA_QK)),
        'l0_mla_kv_a_norm': gain(MLA_KV_RANK),
        'l0_mla_w_kv_up': dense((MLA_KV_RANK, MLA_HEADS * (MLA_NOPE + MLA_V))),
        'l0_mla_q_norm': gain(MLA_QK),
        'l0_mla_k_norm': gain(MLA_QK),
        'l0_w_o': dense((EVEN_OUT, D_MODEL)),
        'l0_ffn_norm': gain(D_MODEL),
        'l0_w_gate': dense((D_MODEL, D_FF)),
        'l0_w_up': dense((D_MODEL, D_FF)),
        'l0_w_down': dense((D_FF, D_MODEL)),
        'l1_attn_norm': gain(D_MODEL),
        'l1_w_in': dense((D_MODEL, ODD_IN)),
        'l1_fox_f_bias': 3.0 + 0.5 * jax.random.normal(next(ks), (FOX_HEADS,), jnp.float32),
        'l1_fox_q_norm': gain(FOX_DIM),
        'l1_fox_k_norm': gain(FOX_DIM),
        'l1_w_o': dense((ODD_OUT, D_MODEL)),
        'l1_ffn_norm': gain(D_MODEL),
        'l1_w_gate': dense((D_MODEL, D_FF)),
        'l1_w_up': dense((D_MODEL, D_FF)),
        'l1_w_down': dense((D_FF, D_MODEL)),
    }

def second_block(x, positions,
              l0_attn_norm, l0_w_in, l0_mla_q_a_norm, l0_mla_w_q_up, l0_mla_kv_a_norm,
              l0_mla_w_kv_up, l0_mla_q_norm, l0_mla_k_norm, l0_w_o,
              l0_ffn_norm, l0_w_gate, l0_w_up, l0_w_down,
              l1_attn_norm, l1_w_in, l1_fox_f_bias, l1_fox_q_norm, l1_fox_k_norm, l1_w_o,
              l1_ffn_norm, l1_w_gate, l1_w_up, l1_w_down):
    mixer_params = (
        (l0_attn_norm, l0_w_in, l0_mla_q_a_norm, l0_mla_w_q_up, l0_mla_kv_a_norm,
         l0_mla_w_kv_up, l0_mla_q_norm, l0_mla_k_norm, l0_w_o),
        (l1_attn_norm, l1_w_in, l1_fox_f_bias, l1_fox_q_norm, l1_fox_k_norm, l1_w_o),
    )
    ffn_params = (
        (l0_ffn_norm, l0_w_gate, l0_w_up, l0_w_down),
        (l1_ffn_norm, l1_w_gate, l1_w_up, l1_w_down),
    )
    for layer in range(DEPTH):
        norm_g, *mp = mixer_params[layer]
        h = rms_norm_2(x, norm_g)
        if layer % 2 == 0:
            x = x + even_mixer(h, positions, *mp)
        else:
            x = x + odd_mixer(h, *mp)
        f_norm, w_gate, w_up, w_down = ffn_params[layer]
        x = x + swiglu(rms_norm_2(x, f_norm), w_gate, w_up, w_down)
    return x


def setup_inputs(seed=0):
    out = dict(first_inputs(seed))
    for name, value in second_inputs(seed + 1).items():
        if name != "x":
            out[name + "_2"] = value
    return out


def reference(
    x, a_norm_g, a_w_in, a_conv_w, a_log, a_dt_bias, a_out_norm_g, a_w_out, kv_norm_g, w_kv,
    b_norm_g, b_w_in, b_w_out, rel_bias, final_norm_g, positions_2, l0_attn_norm_2, l0_w_in_2,
    l0_mla_q_a_norm_2, l0_mla_w_q_up_2, l0_mla_kv_a_norm_2, l0_mla_w_kv_up_2, l0_mla_q_norm_2,
    l0_mla_k_norm_2, l0_w_o_2, l0_ffn_norm_2, l0_w_gate_2, l0_w_up_2, l0_w_down_2,
    l1_attn_norm_2, l1_w_in_2, l1_fox_f_bias_2, l1_fox_q_norm_2, l1_fox_k_norm_2, l1_w_o_2,
    l1_ffn_norm_2, l1_w_gate_2, l1_w_up_2, l1_w_down_2,
):
    x = first_block(
        x, a_norm_g, a_w_in, a_conv_w, a_log, a_dt_bias, a_out_norm_g, a_w_out, kv_norm_g, w_kv,
        b_norm_g, b_w_in, b_w_out, rel_bias, final_norm_g,
    )
    return second_block(
        x, positions_2, l0_attn_norm_2, l0_w_in_2, l0_mla_q_a_norm_2, l0_mla_w_q_up_2,
        l0_mla_kv_a_norm_2, l0_mla_w_kv_up_2, l0_mla_q_norm_2, l0_mla_k_norm_2, l0_w_o_2,
        l0_ffn_norm_2, l0_w_gate_2, l0_w_up_2, l0_w_down_2, l1_attn_norm_2, l1_w_in_2,
        l1_fox_f_bias_2, l1_fox_q_norm_2, l1_fox_k_norm_2, l1_w_o_2, l1_ffn_norm_2, l1_w_gate_2,
        l1_w_up_2, l1_w_down_2,
    )


_drawn_inputs = setup_inputs


def setup_inputs(seed=0):
    import zlib

    import numpy as np

    out = dict(_drawn_inputs(seed))
    spreads = {}
    factors = {'a_norm_g': 4.617,
     'a_out_norm_g': 8.0,
     'kv_norm_g': 8.0,
     'b_norm_g': 8.0,
     'final_norm_g': 4.405,
     'l0_mla_q_a_norm_2': 3.615,
     'l0_mla_q_norm_2': 3.751,
     'l0_mla_k_norm_2': 4.07,
     'l1_fox_k_norm_2': 2.896}
    for name, (base, spread) in spreads.items():
        noise = np.random.default_rng([zlib.crc32(name.encode()), seed]).standard_normal(out[name].shape)
        drawn = base * np.exp(spread * noise) if base else spread * noise
        out[name] = jnp.asarray(drawn.astype(out[name].dtype))
    for name, factor in factors.items():
        out[name] = (out[name] * factor).astype(out[name].dtype)
    return out
```

```python
from contextlib import ExitStack

import concourse.bass as bass
from concourse import mybir

ALU = mybir.AluOpType
ACT = mybir.ActivationFunctionType
AX = mybir.AxisListType
F32 = mybir.dt.float32
F32R = mybir.dt.float32r
I32 = mybir.dt.int32

P = 128
T = 256
NT = T // P
D = 1024
KT = D // P
EPS = 1e-6
NEG = -1e30

CHUNK = 64
HEADS = 8
CONV_W = 4
CONV_T = 3 * KT
N_BUCKETS = 32
MAX_DIST = 2048
MLA_QK, MLA_NOPE, MLA_ROPE = 96, 64, 32
ROPE_THETA = 10000.0
FF = 2816
FT = FF // P
FC = FF // 256

RAW, HIGH, LOW = 4, 2, 2
UNIT = 2048

IDENT, LT, BLK, MNEG, LMT, LM1, CAUSAL, M_UPTO, ONES, STRICT, SBNEG, LE, ANTI, ONEHOT, MINUS, INVF = (
    0, 128, 256, 384, 512, 1280, 1408, 1792, 1920, 2048, 2176, 2304, 2432, 2560, 2944, 3072)
N_CONST = INVF + MLA_ROPE // 2
LEVELS = 6
N_ST = 720
TWO_PI = 6.283185307179586


def shape_constants():
    import math
    import numpy as np
    c = np.zeros((P, N_CONST), np.float32)
    r = np.arange(P)[:, None]
    f = np.arange(P)[None, :]
    same = (r // CHUNK) == (f // CHUNK)
    c[:, IDENT:IDENT + P] = r == f
    c[:, LT:LT + P] = same & (r <= f)
    c[:, BLK:BLK + P] = same
    c[:, MNEG:MNEG + P] = np.where(same & (r <= f), 0.0, NEG)
    for n in range(LEVELS):
        s = 1 << n
        m = (r // (2 * s) == f // (2 * s)) & ((r // s) % 2 == 0) & ((f // s) % 2 == 1)
        c[:, LMT + n * P:LMT + (n + 1) * P] = m
        if n == 0:
            c[:, LM1:LM1 + P] = m.T
    diagonal = np.where(f <= r, 0.0, NEG)
    c[:, CAUSAL:CAUSAL + P] = diagonal
    c[:, CAUSAL + 2 * P:CAUSAL + 3 * P] = diagonal
    c[:, M_UPTO:M_UPTO + P] = -(r >= f).astype(np.float32)
    c[:, MINUS:MINUS + P] = -1.0
    c[:, ONES:ONES + P] = 1.0
    c[:, STRICT:STRICT + P] = r < f
    c[:, SBNEG:SBNEG + P] = np.where(r < f, 0.0, NEG)
    c[:, LE:LE + P] = r <= f
    c[:, ANTI:ANTI + P] = r + f == P - 1
    exact = N_BUCKETS // 2
    for m in range(3 * P - 1):
        n = T - 1 - m
        if n < 0:
            b = N_BUCKETS
        elif n < exact:
            b = n
        else:
            x = np.log(np.float32(n) / np.float32(exact)) / np.float32(math.log(MAX_DIST / exact))
            b = min(exact + int(np.float32(x) * np.float32(N_BUCKETS - exact)), N_BUCKETS - 1)
        c[b, ONEHOT + m] = 1.0
    half = MLA_ROPE // 2
    c[:, INVF:INVF + half] = np.float32(ROPE_THETA) ** (-np.arange(half, dtype=np.float32) / half)
    return c


def block_kernel(nc, A, out):
    ctx = ExitStack()
    with ctx:
        def sb(name, shape, dt=F32, where=None):
            return (where or ctx).enter_context(nc.sbuf_tensor(name, shape, dt))

        sems = {}

        def S(name):
            if name not in sems:
                sems[name] = ctx.enter_context(nc.semaphore(name))
            return sems[name]

        raw = sb("raw", [P, RAW, UNIT])
        whi = sb("whi", [P, HIGH, UNIT], F32R)
        wlo = sb("wlo", [P, LOW, UNIT], F32R)
        x = sb("x", [P, NT, D])
        xn = sb("xn", [P, NT, D])
        xh = sb("xh", [P, KT, T], F32R)
        xl = sb("xl", [P, KT, T], F32R)
        C = sb("C", [P, N_CONST])
        cols = sb("cols", [P, 2, P])
        st = sb("st", [P, N_ST])
        bcs = sb("bcs", [P, 240])
        trig = sb("trig", [P, 2, NT, 16])
        posi = sb("posi", [P, NT], I32)
        ps = ctx.enter_context(nc.psum_tensor("ps", [P, 8, 512], F32))

        lay = ExitStack()
        G = sb("G", [P, 11, UNIT], F32, lay)
        state = sb("state", [P, HEADS, P], F32, lay)
        wab = sb("wab", [P, KT, 16], F32, lay)
        wab_h = sb("wab_h", [P, KT, 16], F32R, lay)
        wab_l = sb("wab_l", [P, KT, 16], F32R, lay)
        lay.close()
        lay = ExitStack()
        bh = sb("bh", [P, KT, T], F32R, lay)
        bl = sb("bl", [P, KT, T], F32R, lay)
        b_kT = sb("b_kT", [P, KT, T], F32, lay)
        b_qT = sb("b_qT", [P, KT, T], F32, lay)
        b_zT = sb("b_zT", [P, KT, T], F32, lay)
        b_v = sb("b_v", [P, NT, D], F32, lay)
        bias_w = sb("bias_w", [P, HEADS, 3 * P], F32, lay)
        bias_r = sb("bias_r", [P, HEADS, T], F32, lay)
        gfin = sb("gfin", [P, D], F32, lay)
        relb = sb("relb", [N_BUCKETS + 1, HEADS], F32, lay)
        brow = sb("brow", [HEADS, 3 * P], F32, lay)
        b_s = sb("b_s", [P, 2, 2, 3 * P], F32, lay)
        b_pT = sb("b_pT", [P, 2, 2, 3 * P], F32, lay)
        b_t = sb("b_t", [P, 2, 2 * T], F32, lay)
        lay.close()
        lay = ExitStack()
        c_in = sb("c_in", [P, NT, 416], F32, lay)
        c_n = sb("c_n", [P, NT, 384], F32, lay)
        ch = sb("ch", [P, 3, T], F32R, lay)
        cl = sb("cl", [P, 3, T], F32R, lay)
        sbT = sb("sbT", [P, KT, T], F32, lay)
        sb_v = sb("sb_v", [P, NT, 512], F32, lay)
        m_qk = sb("m_qk", [P, NT, 16, MLA_QK], F32, lay)
        m_sq = sb("m_sq", [P, NT, 16, MLA_QK], F32, lay)
        m_kv = sb("m_kv", [P, NT, HEADS, P], F32, lay)
        m_qkT = sb("m_qkT", [P, 16, T], F32, lay)
        m_s = sb("m_s", [P, 2, 2, 3 * P], F32, lay)
        m_pT = sb("m_pT", [P, 2, 2, 3 * P], F32, lay)
        sb_e, sb_p = m_s, m_pT
        lay.close()
        ffn = []
        for n in range(2):
            lay = ExitStack()
            ffn.append((sb(f"hTh{n}", [P, FT, T], F32R, lay), sb(f"hTl{n}", [P, FT, T], F32R, lay),
                        sb(f"gate_s{n}", [P, 2, 512], F32, lay), sb(f"hid{n}", [P, 2, 512], F32, lay)))
            lay.close()
        lay = ExitStack()
        f_qk = sb("f_qk", [P, NT, UNIT], F32, lay)
        f_v = sb("f_v", [P, NT, D], F32, lay)
        f_sq = sb("f_sq", [P, NT, UNIT], F32, lay)
        f_qkT = sb("f_qkT", [P, 2 * KT, T], F32, lay)
        f_cT = sb("f_cT", [112, T], F32R, lay)
        f_sel = sb("f_sel", [112, 16, P], F32R, lay)
        f_pick = sb("f_pick", [112, 16], F32, lay)
        wf = sb("wf", [P, KT, 16], F32, lay)
        wf_h = sb("wf_h", [P, KT, 16], F32R, lay)
        wf_l = sb("wf_l", [P, KT, 16], F32R, lay)
        f_s = sb("f_s", [P, 2, 2, 3 * P], F32, lay)
        f_pT = sb("f_pT", [P, 2, 2, 3 * P], F32, lay)
        lay.close()

        ident = C[:, IDENT:IDENT + P]
        abT = G[0:16, 10, 512:512 + T]

        at = [0]

        def small(n):
            at[0] += n
            assert at[0] <= N_ST
            return st[:, at[0] - n:at[0]]

        rms = {}
        for name, n in (("na", 2), ("nb", 2), ("nfin", 2), ("nc", 2), ("nf0", 2), ("nd", 2), ("nf1", 2),
                        ("qk", 32), ("og", 16), ("lat", 4), ("mqk", 32)):
            rms[name] = (small(n), small(n), small(n))
        rms["fqk"] = (cols[:, 0, 0:64], small(64), cols[:, 0, 64:128])
        fox_t, fox_l = small(32), small(32)
        fox_w = f_sq[:, 0, 0:224].rearrange("p (t c) -> p t c", t=NT)
        g_t, g_a, g_e, g_l, g_g, g_b = (small(16) for _ in range(6))
        e_G, e_D, n_G, c_a, c_kb, c_kd = (small(16) for _ in range(6))
        e_C = small(32)

        soft = {n: small(16).rearrange("p (a w t h) -> p a w t h", a=2, w=2, t=NT) for n in ("b", "m", "f")}

        def tok(n):
            return 8 * (n % 2) + n // 2

        causal2 = C[:, CAUSAL:CAUSAL + 3 * P].unsqueeze(1).to_broadcast([P, 2, 3 * P])
        half = lambda t, h: t[64 * (h % 2):64 * (h % 2) + 64]
        attn = {
            "b": dict(heads=HEADS, dv=P, scale=float(P) ** -0.5, q=lambda h: b_qT[:, h], k=lambda h: b_kT[:, h],
                      v=lambda h, kt: b_v[:, kt, P * h:P * h + P], bias=lambda i: bias_w[:, 2 * i:2 * i + 2, :], s=b_s, pT=b_pT),
            "m": dict(heads=HEADS, dv=64, scale=float(MLA_QK) ** -0.5, q=lambda h: m_qkT[0:MLA_QK, h],
                      k=lambda h: m_qkT[0:MLA_QK, HEADS + h], v=lambda h, kt: m_kv[:, kt, h, 64:128],
                      bias=lambda i: causal2, s=m_s, pT=m_pT),
            "f": dict(heads=16, dv=64, scale=0.125, q=lambda h: half(f_qkT[:, h // 2], h),
                      k=lambda h: half(f_qkT[:, KT + h // 2], h), v=lambda h, kt: f_v[:, kt, 64 * h:64 * h + 64],
                      bias=lambda i: causal2, s=f_s, pT=f_pT),
        }

        pair_bank = lambda i: (4, 2)[i % 2]
        SPAN = (slice(0, P), slice(P, 3 * P))

        def pair_out(name, i):
            n = 2 if name == "b" else 1
            return (ps[:, i % 2, 0:n * T].rearrange("p (a t) -> p a t", a=n), slice(n * i, n * i + n))

        conv_col = lambda w, m: cols[:, 0, w * CONV_T + m:w * CONV_T + m + 1]
        r0 = CONV_W * CONV_T
        gain = lambda n: (lambda k: cols[:, n // P, n % P + k:n % P + k + 1])
        gain_a, gain_kv, gain_b, gain_o = gain(r0), gain(r0 + 8), gain(r0 + 16), gain(r0 + 24)
        N_ROWS0 = r0 + 25
        gain_c, gain_f0, gain_d, gain_f1 = gain(P), gain(P + 8), gain(P + 16), gain(P + 24)
        gain_lat, gain_fox = gain(P + 32), gain(P + 35)
        N_ROWS1 = 37
        a_log_b, dt_b, fox_b = bcs[:, 0:8], bcs[:, 8:16], bcs[:, 16:32]
        mla_gain = bcs[:, 32:32 + 192].rearrange("p (a d) -> p a d", a=2)
        rows = G[:, 10, 0:2 * P].rearrange("p (a d) -> p a d", a=2)

        units = []

        def view(name):
            w = A[name]
            if len(w.shape) == 3:
                w = w[0]
            return w.rearrange("(k p) n -> p k n", p=P)

        def std(name, c0, width=512):
            v = view(name)
            for half in range(2):
                units.append((4 * width, [
                    (lambda r, a=a, w=width: r[:, 0:4 * w].rearrange("p (k n) -> p k n", k=4)[:, a:a + 2],
                     v[:, 4 * half + a:4 * half + a + 2, c0:c0 + width]) for a in (0, 2)]))

        def base(emit):
            n = len(units)
            emit()
            return n

        def chunks(name, first, count):
            return lambda: [std(name, 512 * (first + n)) for n in range(count)]

        def gate_up(layer):
            v = [view(f"l{layer}_w_{n}_2") for n in ("gate", "up")]
            for j in range(FC):
                for half in range(2):
                    units.append((UNIT, [
                        (lambda r, a=a: r.rearrange("p (k n) -> p k n", k=4)[:, :, 256 * a:256 * a + 256],
                         v[a][:, 4 * half:4 * half + 4, 256 * j:256 * j + 256]) for a in range(2)]))

        def down(layer):
            v = view(f"l{layer}_w_down_2")
            for u in range(FT // 2):
                units.append((UNIT, [(lambda r, a=a: r[:, D * a:D * a + D], v[:, 2 * u + a, :]) for a in range(2)]))

        def latent_up():
            v = view("l0_mla_w_kv_up_2")
            units.append((1024, [(lambda r, a=a: r[:, 512 * a:512 * a + 512], v[:, 0, 512 * a:512 * a + 512])
                                 for a in range(2)]))
            v = view("l0_mla_w_q_up_2")
            units.append((1536, [(lambda r, a=a: r[:, 768 * a:768 * a + 768], v[:, a, :]) for a in range(2)]))

        U_QKV = base(chunks("a_w_in", 0, 6))
        U_Z = base(chunks("a_w_in", 6, 2))
        U_AO = base(chunks("a_w_out", 0, 2))
        U_BK = base(chunks("w_kv", 0, 2))
        U_BV = base(chunks("w_kv", 2, 2))
        U_BQ = base(chunks("b_w_in", 0, 2))
        U_BZ = base(chunks("b_w_in", 2, 2))
        U_BO = base(chunks("b_w_out", 0, 2))
        U_C = base(lambda: std("l0_w_in_2", 0, 416))
        U_SB = base(lambda: [std("l0_w_in_2", 416 + 512 * n) for n in range(2)])
        U_LAT = base(latent_up)
        U_SV = base(lambda: std("l0_w_in_2", 416 + 1024))
        U_CO = base(chunks("l0_w_o_2", 0, 2))
        U_GU = [base(lambda: gate_up(0))]
        U_DN = [base(lambda: down(0))]
        U_D = base(chunks("l1_w_in_2", 0, 6))
        U_DO = base(chunks("l1_w_o_2", 0, 2))
        U_GU.append(base(lambda: gate_up(1)))
        U_DN.append(base(lambda: down(1)))
        N_UNITS = len(units)

        readers = []

        def readers_of(text):
            readers.extend(text)
            return len(readers) - len(text)

        J_QKV, J_Z, J_AO = readers_of("CCCCCC"), readers_of("AA"), readers_of("DD")
        J_BK, J_BV, J_BQ, J_BZ, J_BO = (readers_of(t) for t in ("AA", "AA", "DD", "AA", "DD"))
        J_C, J_SB, J_LAT, J_SV, J_CO = (readers_of(t) for t in ("D", "AA", "DD", "A", "DD"))
        J_GU = [readers_of("D" * FC)]
        J_DN = [readers_of("DD")]
        J_D, J_DO = readers_of("AAAAAA"), readers_of("DD")
        J_GU.append(readers_of("D" * FC))
        J_DN.append(readers_of("DD"))

        acc_read = {"A": S("acc_read_by_scalar"), "D": S("acc_read_by_vector"), "C": S("conv")}
        raw_in = [S(f"raw_in{n}") for n in range(RAW)]
        hi_done, lo_done, unit_used = S("hi_done"), S("lo_done"), S("unit_used")

        def bank(j):
            return 2 * (j % 2)

        def at_slot(t, g, n, slots):
            return t[:, (g % slots) if isinstance(g, int) else slots, 0:n]

        before, shared = {}, {}

        def share(kind, names, **per_name):
            for what, counts in per_name.items():
                total = 0
                for name, n in zip(names, counts):
                    before[name, what], shared[name, what] = total, f"{kind}_{what}"
                    total += n

        norms, norm_sets = ("na", "nb", "nc", "nf0", "nd", "nf1"), (1, 2, 1, 1, 1, 1)
        share("norm", norms, xn0=[1] * 6, xn1=[1] * 6, T=[4] * 6, hi=[KT * n for n in norm_sets],
              lo=[KT * n for n in norm_sets])
        share("norm", ("na", "nb", "nfin", "nc", "nf0", "nd", "nf1"), ss=[NT] * 7)
        share("root", ("na", "qk", "og", "nb", "nfin", "nc", "lat", "mqk", "nf0", "nd", "fqk", "nf1"),
              mean=[1] * 12, y=[1] * 12, root=[1] * 12)
        share("attn", ("b", "m", "f"), sc=(4, 4, 8), max=(8, 8, 16), exp=(16, 16, 32), p=(8, 8, 16), pT=(4, 4, 8),
              pTs=(4, 4, 8), pv=(4, 4, 8), out_hi=(4, 4, 8), out=(4, 4, 8))
        share("ff", ("ff0", "ff1"), gate=(FC, FC), hi=(FC, FC), lo=(FC, FC))

        def step(name, what):
            return S(shared[name, what])

        def past(name, what, n):
            return S(shared[name, what]), n + before[name, what]

        scratch = nc.dram_tensor("bias_rows", (HEADS, 3 * P), F32, kind="Internal").ap()

        o_tile = lambda tt: G[:, 4, :].rearrange("p (h t d) -> p h t d", h=HEADS, t=NT)[:, :, tt, :]
        o_sq = lambda tt: G[:, 7, :].rearrange("p (h t d) -> p h t d", h=HEADS, t=NT)[:, :, tt, :]

        def read_by(e, j):
            return readers[:j + 1].count(e)

        def row_dma(e, n, name, k):
            v = A[name]
            v = v[0] if len(v.shape) == 2 else v
            e.dma_start(rows[n % P:n % P + k, n // P, :], v.rearrange("(k p) -> k p", p=P)).then_inc(S("rows_in"), 16)

        block = ctx.enter_context(nc.Block())

        @block.sync
        def _(sp):
            def load(g, slot, work, more=0):
                for to, src in work:
                    sp.dma_start(to(raw[:, slot, :]), src).then_inc(raw_in[slot], 16)

            for a in (slice(IDENT, IDENT + P), slice(INVF, N_CONST)):
                sp.dma_start(C[:, a], A["consts"][:, a]).then_inc(S("const_in"), 16)
            for tt in range(NT):
                sp.dma_start(x[:, tt, :], A["x"][0, tt * P:(tt + 1) * P, :]).then_inc(S("x_in"), 16)
            for n, name, k in ((P, "l0_attn_norm_2", 8), (P + 8, "l0_ffn_norm_2", 8),
                               (P + 16, "l1_attn_norm_2", 8), (P + 24, "l1_ffn_norm_2", 8),
                               (P + 32, "l0_mla_q_a_norm_2", 2), (P + 34, "l0_mla_kv_a_norm_2", 1)):
                row_dma(sp, n, name, k)
            for n, name in enumerate(("l1_fox_q_norm_2", "l1_fox_k_norm_2")):
                for a in range(2):
                    sp.dma_start(rows[35 + n:36 + n, 1, 64 * a:64 * a + 64],
                                 A[name].rearrange("(a p) -> a p", a=1)).then_inc(S("rows_in"), 16)
            sp.wait_ge(S("rows_in"), 16 * 15)
            for g in range(2):
                load(g, g, units[g][1])
            sp.dma_start(C[:, IDENT + P:INVF], A["consts"][:, IDENT + P:INVF]).then_inc(S("masks_in"), 16)
            g = 2
            while g < N_UNITS:
                if g in U_GU:
                    layer = U_GU.index(g)
                    v = [view(f"l{layer}_w_{n}_2") for n in ("gate", "up")]
                    with sp.Fori(0, FC // 2) as i:
                        for c in range(4):
                            sp.wait_ge(lo_done, i * 4 + (g + c - RAW + 1))
                            slot = (g + c) % RAW
                            r = raw[:, slot, :].rearrange("p (k n) -> p k n", k=4)
                            for a in range(2):
                                sp.dma_start(r[:, :, 256 * a:256 * a + 256],
                                             v[a][:, 4 * (c % 2):4 * (c % 2) + 4,
                                                  bass.ds(i * 512 + 256 * (c // 2), 256)]).then_inc(raw_in[slot], 16)
                    g += 4 * (FC // 2)
                    continue
                if g >= RAW:
                    sp.wait_ge(lo_done, g - RAW + 1)
                load(g, g % RAW, units[g][1])
                g += 1
            for n in range(NT):
                sp.wait_ge(S("final_x"), n + 1)
                sp.dma_start(out[0, :, 512 * n:512 * (n + 1)].rearrange("(t p) d -> p t d", p=P),
                             x[:, :, 512 * n:512 * (n + 1)]).then_inc(S("out_done"), 16)
            sp.wait_ge(S("out_done"), 16 * NT)

        @block.gpsimd
        def _(pool):
            with nc.allow_non_contiguous_dma(reason="256 positions"):
                pool.dma_start(posi[:], A["positions_2"].rearrange("a (t p) -> p (a t)", p=P)).then_inc(S("pos_in"), 16)
            pool.dma_start(wab[:], view("a_w_in")[:, :, 4096:4112]).then_inc(S("wab_in"), 16)
            for to, name, n in ((a_log_b, "a_log", 8), (dt_b, "a_dt_bias", 8), (fox_b, "l1_fox_f_bias_2", 16),
                                (mla_gain[:, 0, :], "l0_mla_q_norm_2", MLA_QK),
                                (mla_gain[:, 1, :], "l0_mla_k_norm_2", MLA_QK)):
                pool.dma_start(to, bass.AP(A[name].tensor, 0, [[0, P], [1, n]])).then_inc(S("spread_in"), 16)
            pool.wait_ge(S("masks_in"), 16)
            for q in range(4):
                pool.wait_ge(S("d_egb"), q + 1)
                a = slice(512 * q, 512 * q + 512)
                nc.gpsimd.tensor_tensor(G[:, 5, a], G[:, 5, a], G[:, 0, a], ALU.mult).then_inc(S("d_qdec"), 1)
            pool.wait_ge(S("o_gated"), NT)
            nc.gpsimd.memset(relb[N_BUCKETS:N_BUCKETS + 1, :], NEG).then_inc(S("relb_mask"), 1)
            pool.dma_start(relb[0:N_BUCKETS, :], A["rel_bias"]).then_inc(S("relb_in"), 16)
            pool.dma_start(gfin[:], bass.AP(A["final_norm_g"].tensor, 0, [[0, P], [1, D]])).then_inc(S("gfin_in"), 16)
            pool.wait_ge(S("brow_copied"), 2)
            pool.dma_start(scratch, brow[:]).then_inc(S("scratch"), 16)
            pool.wait_ge(S("scratch"), 16)
            pool.dma_start(bias_r[:], bass.AP(scratch.tensor, 0, [[1, P], [3 * P, HEADS], [1, T]])).then_inc(S("bias_in"), 16)
            pool.wait_ge(acc_read["D"], read_by("D", J_C))
            for tt in range(NT):
                nc.gpsimd.tensor_copy(m_qk[:, tt, 8:16, MLA_NOPE:MLA_QK],
                                      c_in[:, tt, 384:416].unsqueeze(1).to_broadcast([P, 8, MLA_ROPE])).then_inc(S("k_rope"), 1)
            links = [0]

            def link(ins):
                links[0] += 1
                ins.then_inc(S("pool_chain"), 1)
                pool.wait_ge(S("pool_chain"), links[0])

            pool.wait_ge(*past("mqk", "root", 1))
            mq = m_qk[:].rearrange("p t h d -> p (t h) d")
            link(nc.gpsimd.tensor_tensor(mq, mq, rms["mqk"][1].unsqueeze(2).to_broadcast([P, 32, MLA_QK]), ALU.mult))
            pool.wait_ge(S("spread_in"), 80)
            for n in range(2):
                part = m_qk[:, :, 8 * n:8 * n + 8, :]
                link(nc.gpsimd.tensor_tensor(part, part, mla_gain[:, n, :].unsqueeze(1).unsqueeze(1)
                                             .to_broadcast([P, NT, 8, MLA_QK]), ALU.mult))
            pool.wait_ge(S("trig"), 2)
            r1, r2 = m_qk[:, :, :, 64:80], m_qk[:, :, :, 80:96]
            flat = m_sq[:].rearrange("p t h d -> p (t h d)")
            t4 = [flat[:, 512 * n:512 * n + 512].rearrange("p (t h d) -> p t h d", t=NT, h=16) for n in range(4)]
            sin, cos = (trig[:, n].unsqueeze(2).to_broadcast([P, NT, 16, 16]) for n in range(2))
            for o_, a, b in zip(t4, (r1, r2, r2, r1), (cos, sin, cos, sin)):
                nc.gpsimd.tensor_tensor(o_, a, b, ALU.mult).then_inc(S("rope_t"), 1)
            pool.wait_ge(S("rope_t"), 4)
            nc.gpsimd.tensor_tensor(r1, t4[0], t4[1], ALU.subtract).then_inc(S("rope"), 1)
            nc.gpsimd.tensor_tensor(r2, t4[2], t4[3], ALU.add).then_inc(S("rope"), 1)
            pool.wait_ge(acc_read["D"], read_by("D", J_DN[0] + 1))
            nc.gpsimd.tensor_copy(f_pick[:], C[0:112, IDENT:IDENT + 16]).then_inc(S("f_pick"), 1)
            for n in range(1, 4):
                pool.wait_ge(S("f_pick"), n)
                nc.gpsimd.tensor_tensor(f_pick[:], f_pick[:], C[0:112, IDENT + 32 * n:IDENT + 32 * n + 16], ALU.add)\
                    .then_inc(S("f_pick"), 1)
            pool.wait_ge(S("f_pick"), 4)
            nc.gpsimd.tensor_copy(f_sel[:], f_pick[:].unsqueeze(2).to_broadcast([112, 16, P])).then_inc(S("f_sel"), 1)
            pool.wait_ge(*past("fqk", "root", 1))
            nc.gpsimd.tensor_tensor(f_qk[:, 1, :].rearrange("p (h d) -> p h d", d=64),
                                    f_qk[:, 1, :].rearrange("p (h d) -> p h d", d=64),
                                    rms["fqk"][1][:, 32:64].unsqueeze(2).to_broadcast([P, 32, 64]), ALU.mult)\
                .then_inc(S("f_scaled1"), 1)

        @block.scalar
        def _(act):
            emitted = [0]

            def hi(g, slots=None, i=None):
                n = units[g][0]
                if i is None:
                    act.wait_ge(raw_in[g % RAW], 32 * (g // RAW + 1))
                    if g >= HIGH:
                        act.wait_ge(unit_used, g - HIGH + 1)
                else:
                    act.wait_ge(raw_in[g % RAW], i * (32 * 4 // RAW) + 32 * (g // RAW + 1))
                    act.wait_ge(unit_used, i * 4 + (g - HIGH + 1))
                nc.scalar.activation(whi[:, g % HIGH, 0:n], raw[:, g % RAW, 0:n], ACT.Copy).then_inc(hi_done, 1)

            def hi_until(g):
                while emitted[0] < min(g, N_UNITS):
                    hi(emitted[0])
                    emitted[0] += 1

            chain = [0]

            def link(ins):
                chain[0] += 1
                ins.then_inc(S("act_chain"), 1)
                act.wait_ge(S("act_chain"), chain[0])

            def root(name):
                ms, y, _ = rms[name]
                act.wait_ge(*past(name, "mean", 1))
                link(nc.scalar.activation(y, ms, ACT.Ln))
                nc.scalar.activation(y, y, ACT.Exp, scale=-0.5).then_inc(step(name, "y"), 1)

            def norm(name, sets, wait, ahead):
                ms, y, _ = rms[name]
                for tt in range(NT):
                    wait(tt)
                    nc.scalar.activation(xn[:, tt, :], x[:, tt, :], ACT.Square,
                                         accum_out=ms[:, tt:tt + 1]).then_inc(step(name, "ss"), 1)
                root(name)
                act.wait_ge(*past(name, "root", 1))
                nc.scalar.activation(xn[:, 1, :], x[:, 1, :], ACT.Copy, scale=y[:, 1:2]).then_inc(step(name, "xn1"), 1)
                hi_until(ahead)
                if name == "na":
                    act.wait_ge(S("cols_done"), 2)
                for n, (g_, h_, _) in enumerate(sets):
                    for b in range(4):
                        act.wait_ge(*past(name, "T", b + 1))
                        if n:
                            act.wait_ge(*past(name, "lo", KT * (n - 1) + 2 * b + 2))
                        for k in (2 * b, 2 * b + 1):
                            nc.scalar.activation(h_[:, k], ps[:, 4 + b, 256 * (k % 2):256 * (k % 2) + 256], ACT.Copy,
                                                 scale=g_(k)).then_inc(step(name, "hi"), 1)

            def softmax(name):
                w = attn[name]
                mx, pairs = soft[name], w["heads"] // 2
                for i in range(pairs + 3):
                    h = i - 2
                    if 0 <= h < pairs:
                        act.wait_ge(*past(name, "pT", h + 1))
                        if h >= 2:
                            act.wait_ge(*past(name, "pv", h - 1))
                        nc.scalar.activation(w["pT"][:, h % 2], ps[:, 6:8, 0:3 * P],
                                             ACT.Copy).then_inc(step(name, "pTs"), 1)
                    if i < pairs:
                        act.wait_ge(*past(name, "max", 2 * (i + 1)))
                        for tt in range(NT):
                            for n in range(2):
                                s_ = w["s"][:, i % 2, n, SPAN[tt]]
                                nc.scalar.activation(s_, s_, ACT.Exp, bias=mx[:, i % 2, 0, tt, n:n + 1],
                                                     accum_out=mx[:, i % 2, 1, tt, n:n + 1])\
                                    .then_inc(step(name, "exp"), 1)
                    h = i - 3
                    if h >= 0:
                        src, to = pair_out(name, h)
                        if name == "b":
                            act.wait_ge(S("b_gated"), h + 1)
                            src = b_t[:, h % 2, :].rearrange("p (a t) -> p a t", a=2)
                        else:
                            act.wait_ge(*past(name, "pv", h + 1))
                        nc.scalar.activation(xh[:, to], src, ACT.Copy).then_inc(step(name, "out_hi"), 1)

            def ln_exp():
                nc.scalar.preload_act_table_set("natural_log_exp_and_others")

            act.dma_start(rows[0:r0, 0, :], A["a_conv_w"][0].rearrange("w (m p) -> (w m) p", p=P)).then_inc(S("rows_in"), 16)
            for n, name, k in ((r0, "a_norm_g", 8), (r0 + 8, "kv_norm_g", 8), (r0 + 16, "b_norm_g", 8),
                               (r0 + 24, "a_out_norm_g", 1)):
                row_dma(act, n, name, k)

            for n in range(2):
                act.wait_ge(S("trig_arg"), n + 1)
                nc.scalar.activation(trig[:, n], trig[:, n], ACT.Sin).then_inc(S("trig"), 1)
            ln_exp()
            norm("na", [(gain_a, xh, xl)],
                 lambda tt: act.wait_ge(S("x_in"), 32), U_QKV + 1)
            act.wait_ge(S("wab_in"), 16)
            nc.scalar.activation(wab_h[:], wab[:], ACT.Copy).then_inc(S("wab_hi"), 1)

            hi_until(U_QKV + 1)

            def silu_qkv(c):
                act.wait_ge(S("conv"), 12 * (c + 1))
                v = G[:, c // 2, 1024 * (c % 2):1024 * (c % 2) + 1024]
                nc.scalar.activation(v, v, ACT.Silu).then_inc(S("qkv"), 1)
                if c < 4:
                    act.wait_ge(S("qkv"), c + 1)
                    if c == 1:
                        act.wait_ge(S("abT"), 1)
                        nc.scalar.activation(abT, ps[0:16, 6, 0:T], ACT.Copy).then_inc(S("ab_sb"), 1)
                    nc.scalar.activation(G[:, 6 + c // 2, 1024 * (c % 2):1024 * (c % 2) + 1024], v,
                                         ACT.Square).then_inc(S("qk_sq"), 1)

            for c in range(6):
                hi_until(U_QKV + 2 * c + 4)
                act.wait_ge(unit_used, U_QKV + 2 * c + 2)
                if c == 5:
                    hi_until(U_Z + 2)
                for m in range(4):
                    t_ = 4 * c + m
                    nc.scalar.activation(G[:, t_ // 8, 256 * (t_ % 8):256 * (t_ % 8) + 256],
                                         ps[:, bank(J_QKV + c) + m // 2, 256 * (m % 2):256 * (m % 2) + 256],
                                         ACT.Copy, scale=conv_col(3, t_)).then_inc(S("tap3"), 1)
                if c >= 1:
                    silu_qkv(c - 1)
            silu_qkv(5)
            def silu_z(c):
                act.wait_ge(unit_used, U_Z + 2 * c + 2)
                nc.scalar.activation(G[:, 3, :].rearrange("p (t n) -> p t n", t=NT)[:, :, 512 * c:512 * c + 512],
                                     ps[:, bank(J_Z + c):bank(J_Z + c) + 2, :], ACT.Silu).then_inc(acc_read["A"], 1)

            hi_until(U_Z + 3)
            silu_z(0)
            hi_until(U_Z + 4)
            ln_exp()
            root("qk")
            act.wait_ge(S("spread_in"), 80)
            act.wait_ge(S("gate_t"), 1)
            link(nc.scalar.activation(g_a, g_t, ACT.Abs))
            link(nc.scalar.activation(g_e, g_a, ACT.Exp, scale=-1.0))
            nc.scalar.activation(g_l, g_e, ACT.Ln, bias=1.0).then_inc(S("gate_l"), 1)
            nc.scalar.activation(a_log_b, a_log_b, ACT.Exp).then_inc(S("gate_l"), 1)
            nc.scalar.activation(g_b.rearrange("p (t h) -> p t h", t=NT), ps[:, 6, 256:288].rearrange("p (t h) -> p t h", t=NT)[:, :, 8:16], ACT.Exp,
                                 scale=-1.0).then_inc(S("gate_l"), 1)
            act.wait_ge(S("gsum"), 1)
            act.wait_ge(S("gdiff"), 1)
            nc.scalar.activation(e_G, ps[:, 5, 0:16], ACT.Exp).then_inc(S("gexp"), 1)
            nc.scalar.activation(e_D, e_D, ACT.Exp).then_inc(S("gexp"), 1)
            nc.scalar.activation(e_C, ps[:, 5, 32:64], ACT.Exp).then_inc(S("gexp"), 1)
            for q_ in range(4):
                act.wait_ge(S("d_arg"), 4 * q_ + 4)
                nc.scalar.activation(G[:, 5, 512 * q_:512 * q_ + 512], ps[:, 4 + q_, :], ACT.Exp).then_inc(S("d_egb"), 1)
                a = slice(512 * q_, 512 * q_ + 512)
                nc.scalar.activation(G[:, 4, a], G[:, 4, a], ACT.Exp).then_inc(S("decay"), 1)
            act.wait_ge(S("gscale"), 1)
            for q_ in range(4):
                act.wait_ge(S("k_tm"), q_ + 1)
                for n in range(4 * q_, 4 * q_ + 4):
                    act_n = tok(n)
                    nc.scalar.activation(G[:, 6, P * n:P * n + P], ps[:, 4 + q_, P * (n % 4):P * (n % 4) + P],
                                         ACT.Copy, scale=c_kd[:, act_n:act_n + 1]).then_inc(S("kd"), 1)
            for q_ in range(4):
                act.wait_ge(S("v_tm"), q_ + 1)
                for n in range(4 * q_, 4 * q_ + 4):
                    nc.scalar.activation(G[:, 2, P * n:P * n + P], ps[:, 4 + q_, P * (n % 4):P * (n % 4) + P],
                                         ACT.Copy, scale=g_b[:, tok(n):tok(n) + 1]).then_inc(S("vb"), 1)
            for q_ in range(4):
                act.wait_ge(S("s_t"), q_ + 1)
                for n in range(4 * q_, 4 * q_ + 4):
                    nc.scalar.activation(G[:, 4, P * n:P * n + P], ps[:, q_, P * (n % 4):P * (n % 4) + P],
                                         ACT.Copy, scale=c_a[:, tok(n):tok(n) + 1]).then_inc(S("a_mat"), 1)
            for q_ in range(4):
                act.wait_ge(S("u_ps"), q_ + 1)
                nc.scalar.activation(G[:, 10, 512 * q_:512 * q_ + 512], ps[:, q_, :], ACT.Copy).then_inc(S("u"), 1)
            for tt in range(NT):
                act.wait_ge(S("o"), 4 * (tt + 1))
                nc.scalar.activation(o_sq(tt), o_tile(tt), ACT.Square).then_inc(S("o_sq"), 1)
            root("og")
            nc.scalar.preload_act_table(ACT.Silu)
            hi_until(U_AO + 1)
            silu_z(1)
            for b in range(4):
                if b == 2:
                    hi_until(U_AO + 2)
                act.wait_ge(S("oT"), b + 1)
                nc.scalar.activation(xh[:, 2 * b:2 * b + 2, :], ps[:, 4 + b, :].rearrange("p (a t) -> p a t", a=2),
                                     ACT.Copy, scale=gain_o(0)).then_inc(S("oT_hi"), 1)
            hi_until(U_AO + 5)

            def evacuate(u0, j0, c, to, func=ACT.Copy, **kw):
                act.wait_ge(unit_used, u0 + 2 * c + 2)
                nc.scalar.activation(to, ps[:, bank(j0 + c):bank(j0 + c) + 2, :], func, **kw).then_inc(acc_read["A"], 1)

            fm_tiles = lambda t, c: t[:, 4 * c:4 * c + 4, :].rearrange("p (a m) t -> p a (m t)", a=2)
            norm("nb", [(gain_kv, xh, xl), (gain_b, bh, bl)], lambda tt: act.wait_ge(acc_read["D"], read_by("D", J_AO + 1)),
                 U_BK + 2)
            hi_until(U_BK + 2)
            for c in range(2):
                hi_until(U_BK + 2 * c + 4)
                evacuate(U_BK, J_BK, c, fm_tiles(b_kT, c))
            for c in range(2):
                hi_until(U_BV + 2 * c + 4)
                evacuate(U_BV, J_BV, c, b_v[:, :, 512 * c:512 * c + 512])
            for c in range(2):
                hi_until(U_BQ + 2 * c + 4)
                act.wait_ge(S("bias_ps"), 4)
                for b in (2 * c, 2 * c + 1):
                    src = ps[:, 4 + b, :].rearrange("p (h k) -> p h k", h=2)
                    nc.scalar.activation(bias_w[:, 2 * b:2 * b + 2, P:3 * P], src, ACT.Copy).then_inc(S("bias_w"), 1)
                    nc.scalar.activation(bias_w[:, 2 * b:2 * b + 2, 0:P], src[:, :, P:T], ACT.Copy).then_inc(S("bias_w"), 1)
            for c in range(2):
                hi_until(U_BZ + 2 * c + 4)
                evacuate(U_BZ, J_BZ, c, fm_tiles(b_zT, c), ACT.Silu)
            hi_until(U_BO + 2)
            ln_exp()
            softmax("b")
            hi_until(U_BO + 5)
            act.wait_ge(acc_read["D"], read_by("D", J_BO + 1))
            for tt in range(NT):
                nc.scalar.activation(xn[:, tt, :], x[:, tt, :], ACT.Square,
                                     accum_out=rms["nfin"][0][:, tt:tt + 1]).then_inc(step("nfin", "ss"), 1)
            root("nfin")

            norm("nc", [(gain_c, xh, xl)], lambda tt: act.wait_ge(S("x_first"), tt + 1), U_C + 2)
            hi_until(U_C + 3)
            act.wait_ge(acc_read["D"], read_by("D", J_C))
            for n, (a, b) in enumerate(((0, 256), (256, 384))):
                for tt in range(NT):
                    k = 2 * n + tt
                    nc.scalar.activation(c_n[:, tt, a:b], c_in[:, tt, a:b], ACT.Square,
                                         accum_out=rms["lat"][0][:, k:k + 1]).then_inc(S("lat_ss"), 1)
            root("lat")
            hi_until(U_SB + 3)
            evacuate(U_SB, J_SB, 0, fm_tiles(sbT, 0), scale=0.125)
            for k in range(3):
                act.wait_ge(S("lat_T"), k // 2 + 1)
                nc.scalar.activation(ch[:, k], ps[:, 4 + k // 2, 256 * (k % 2):256 * (k % 2) + 256], ACT.Copy,
                                     scale=gain_lat(k)).then_inc(S("lat_hi"), 1)
            hi_until(U_SB + 5)
            evacuate(U_SB, J_SB, 1, fm_tiles(sbT, 1))
            hi_until(U_LAT + 2)
            act.wait_ge(unit_used, U_LAT + 1)
            for tt in range(NT):
                kv = ps[:, 4 + 2 * tt:6 + 2 * tt, :].rearrange("p b (h d) -> p (b h) d", d=P)
                nc.scalar.activation(m_qk[:, tt, 8:16, 0:MLA_NOPE], kv[:, :, 0:64], ACT.Copy).then_inc(S("kv_read"), 1)
                nc.scalar.activation(m_kv[:, tt, :, 64:128], kv[:, :, 64:128], ACT.Copy).then_inc(S("kv_read"), 1)
            hi_until(U_SV + 2)
            act.wait_ge(S("k_rope"), NT)
            act.wait_ge(S("kv_read"), 2 * NT)
            act.wait_ge(acc_read["D"], read_by("D", J_LAT + 1))
            for tt in range(NT):
                nc.scalar.activation(m_sq[:, tt], m_qk[:, tt], ACT.Square).then_inc(S("m_sq"), 1)
            root("mqk")
            hi_until(U_SV + 3)
            evacuate(U_SV, J_SV, 0, sb_v[:])
            for i in range(HEADS // 2 + 2):
                if i < HEADS // 2:
                    b, e_ = pair_bank(i), sb_e[:, i % 2]
                    act.wait_ge(S("sb_z"), i + 1)
                    if i >= 2:
                        act.wait_ge(S("sb_p"), i - 1)
                    link(nc.scalar.activation(e_, ps[:, b:b + 2, 0:3 * P], ACT.Abs))
                    link(nc.scalar.activation(e_, e_, ACT.Exp, scale=-1.0))
                    nc.scalar.activation(e_, e_, ACT.Ln, bias=1.0).then_inc(S("sb_l"), 1)
                g = i - 1
                if 0 <= g < HEADS // 2:
                    act.wait_ge(S("sb_arg"), g + 1)
                    if g >= 2:
                        act.wait_ge(S("sb_pv"), g - 1)
                    nc.scalar.activation(sb_p[:, g % 2], ps[:, pair_bank(g):pair_bank(g) + 2, 0:3 * P], ACT.Exp).then_inc(S("sb_p"), 1)
                g = i - 2
                if g >= 0:
                    act.wait_ge(S("sb_pv"), g + 1)
                    nc.scalar.activation(xh[:, 4 + g], ps[:, g % 2, 0:T], ACT.Copy).then_inc(S("sb_out_hi"), 1)
            for f in range(0, 8, 2):
                act.wait_ge(S("m_T"), f + 1)
                nc.scalar.activation(m_qkT[0:MLA_QK, 2 * f:2 * f + 2, :].rearrange("p a t -> p (a t)"),
                                     ps[0:MLA_QK, 4 + f % 4, :], ACT.Copy).then_inc(S("m_Ts_a"), 1)
            hi_until(U_CO + 2)
            softmax("m")
            hi_until(U_CO + 5)

            def feed_forward(n, name, g_, j_before):
                norm(name, [(g_, xh, xl)], lambda tt: act.wait_ge(acc_read["D"], read_by("D", j_before + 1)),
                     U_GU[n] + 2)
                hi_until(U_GU[n] + 2)
                b, gs = U_GU[n], ffn[n][2]

                def gate(c, i=None):
                    act.wait_ge(unit_used, b + 2 * c + 2 if i is None else i * 4 + (b + 2 * c + 2))
                    nc.scalar.activation(gs[:, c % 2, :], ps[:, bank(J_GU[n] + c), :], ACT.Silu)\
                        .then_inc(step(f"ff{n}", "gate"), 1)

                nc.scalar.preload_act_table(ACT.Silu)
                with act.Fori(0, FC // 2) as i:
                    for c in range(2):
                        hi(b + 2 * c + 2, i=i)
                        hi(b + 2 * c + 3, i=i)
                        gate(c, i)
                emitted[0] += 4 * (FC // 2)
                hi_until(b + 2 * FC + 2)
                gate(FC - 1)
                hi_until(U_DN[n] + FT // 2 + 1)

            feed_forward(0, "nf0", gain_f0, J_CO)

            ln_exp()
            norm("nd", [(gain_d, xh, xl)], lambda tt: act.wait_ge(acc_read["D"], read_by("D", J_DN[0] + 1)),
                 U_D + 2)
            act.dma_start(wf[:], view("l1_w_in_2")[:, :, 3072:3088]).then_inc(S("wf_in"), 16)
            hi_until(U_D + 2)
            for c in range(6):
                hi_until(U_D + 2 * c + 4)
                if c < 4:
                    evacuate(U_D, J_D, c, f_qk[:, :, 512 * c:512 * c + 512])
                    act.wait_ge(acc_read["A"], read_by("A", J_D + c))
                    nc.scalar.activation(f_sq[:, :, 512 * c:512 * c + 512], f_qk[:, :, 512 * c:512 * c + 512],
                                         ACT.Square).then_inc(S("f_sq"), 1)
                else:
                    evacuate(U_D, J_D, c, f_v[:, :, 512 * (c - 4):512 * (c - 4) + 512])
                    if c == 4:
                        root("fqk")
                        act.wait_ge(S("f_logit"), 1)
                        link(nc.scalar.activation(fox_l, fox_t, ACT.Abs))
                        link(nc.scalar.activation(fox_l, fox_l, ACT.Exp, scale=-1.0))
                        nc.scalar.activation(fox_l, fox_l, ACT.Ln, bias=1.0).then_inc(S("f_l"), 1)
                if c == 0:
                    act.wait_ge(S("wf_in"), 16)
                    nc.scalar.activation(wf_h[:], wf[:], ACT.Copy).then_inc(S("wf_hi"), 1)
            for f in range(0, 8, 2):
                act.wait_ge(S("f_T"), f + 1)
                nc.scalar.activation(f_qkT[:, 2 * f:2 * f + 2, :].rearrange("p a t -> p (a t)"), ps[:, 4 + f % 4, :],
                                     ACT.Copy, scale=gain_fox(f // 4)).then_inc(S("f_Ts_a"), 1)
            hi_until(U_DO + 2)
            softmax("f")
            hi_until(U_DO + 5)
            feed_forward(1, "nf1", gain_f1, J_DO)

        @block.vector
        def _(dve):
            emitted = [0]

            def lo(g, i=None):
                n = units[g][0]
                dve.wait_ge(hi_done, g + 1 if i is None else i * 4 + (g + 1))
                if i is not None or g >= LOW:
                    dve.wait_ge(unit_used, g - LOW + 1 if i is None else i * 4 + (g - LOW + 1))
                nc.vector.tensor_tensor(wlo[:, g % LOW, 0:n], raw[:, g % RAW, 0:n],
                                        whi[:, g % HIGH, 0:n].bitcast(F32), ALU.subtract).then_inc(lo_done, 1)

            def lo_until(g):
                while emitted[0] < min(g, N_UNITS):
                    lo(emitted[0])
                    emitted[0] += 1

            chain = [0]

            def link(ins):
                chain[0] += 1
                ins.then_inc(S("dve_chain"), 1)
                dve.wait_ge(S("dve_chain"), chain[0])

            def mean(name, src, n, over):
                ms = rms[name][0]
                nc.vector.tensor_scalar(ms, src, 1.0 / over, EPS, ALU.mult, ALU.add).then_inc(step(name, "mean"), 1)

            def refine(name):
                ms, y, t = rms[name]
                dve.wait_ge(*past(name, "y", 1))
                link(nc.vector.scalar_tensor_tensor(t, y, -0.5, y, ALU.mult, ALU.mult))
                link(nc.vector.tensor_tensor(t, t, ms, ALU.mult))
                nc.vector.scalar_tensor_tensor(y, t, 1.5, y, ALU.add, ALU.mult).then_inc(step(name, "root"), 1)
                dve.wait_ge(*past(name, "root", 1))

            def norm(name, sets, ahead):
                ms, y, _ = rms[name]
                dve.wait_ge(*past(name, "ss", NT))
                mean(name, ms, 2, D)
                refine(name)
                nc.vector.tensor_scalar(xn[:, 0, :], x[:, 0, :], y[:, 0:1], None, ALU.mult).then_inc(step(name, "xn0"), 1)
                lo_until(ahead)
                for n, (g_, h_, l_) in enumerate(sets):
                    for k in range(KT):
                        dve.wait_ge(*past(name, "hi", KT * n + 2 * (k // 2 + 1)))
                        nc.vector.scalar_tensor_tensor(
                            l_[:, k], ps[:, 4 + k // 2, 256 * (k % 2):256 * (k % 2) + 256], g_(k),
                            h_[:, k].bitcast(F32), ALU.mult, ALU.subtract).then_inc(step(name, "lo"), 1)

            def residual(u0, j0):
                for c in range(2):
                    lo_until(u0 + 2 * c + (3 if c else 4))
                    dve.wait_ge(unit_used, u0 + 2 * c + 2)
                    xs = x[:, :, 512 * c:512 * c + 512]
                    nc.vector.tensor_tensor(xs, xs, ps[:, bank(j0 + c):bank(j0 + c) + 2, :], ALU.add)\
                        .then_inc(acc_read["D"], 1)

            ang, turns, rest = (G[:, 9, 32 * n:32 * n + 32].rearrange("p (t n) -> p t n", t=NT) for n in range(3))
            posf = G[:, 9, 96:98]
            dve.wait_ge(S("pos_in"), 16)
            link(nc.vector.tensor_copy(posf, posi[:]))
            dve.wait_ge(S("const_in"), 32)
            link(nc.vector.tensor_tensor(ang, posf.unsqueeze(2).to_broadcast([P, NT, 16]),
                                         C[:, INVF:INVF + 16].unsqueeze(1).to_broadcast([P, NT, 16]), ALU.mult))
            MAGIC = 12582912.0
            link(nc.vector.tensor_scalar(turns, ang, 1.0 / TWO_PI, MAGIC, ALU.mult, ALU.add))
            link(nc.vector.tensor_scalar(turns, turns, MAGIC, None, ALU.subtract))
            link(nc.vector.scalar_tensor_tensor(rest, turns, -6.28125, ang, ALU.mult, ALU.add))
            link(nc.vector.scalar_tensor_tensor(rest, turns, -1.93500518798828125e-3, rest, ALU.mult, ALU.add))
            link(nc.vector.scalar_tensor_tensor(rest, turns, -(TWO_PI - 6.28125 - 1.93500518798828125e-3), rest,
                                                ALU.mult, ALU.add))
            PI = 3.1415925
            nc.vector.tensor_scalar(trig[:, 0], rest, PI, -PI, ALU.min, ALU.max).then_inc(S("trig_arg"), 1)
            link(nc.vector.tensor_scalar(turns, rest, -1.0, None, ALU.mult))
            link(nc.vector.tensor_tensor(turns, turns, rest, ALU.max))
            nc.vector.tensor_scalar(trig[:, 1], turns, -1.0, TWO_PI / 4, ALU.mult, ALU.add).then_inc(S("trig_arg"), 1)
            for b, n in ((0, N_ROWS0), (1, N_ROWS1)):
                dve.wait_ge(S("rows_T"), b + 1)
                nc.vector.tensor_copy(cols[:, b, 0:n], ps[:, 4 + b, 0:n]).then_inc(S("cols_done"), 1)
            norm("na", [(gain_a, xh, xl)], U_QKV + 1)
            dve.wait_ge(S("wab_hi"), 1)
            nc.vector.tensor_tensor(wab_l[:], wab[:], wab_h[:].bitcast(F32), ALU.subtract).then_inc(S("wab_lo"), 1)

            dve.wait_ge(S("masks_in"), 16)
            lo_until(U_QKV + 1)
            for c in range(6):
                lo_until(U_QKV + 2 * c + 4)
                for back in (1, 2, 3):
                    for m in range(4):
                        t_ = 4 * c + m
                        if back == 1:
                            if c == 5 and m == 0:
                                lo_until(U_Z + 2)
                            dve.wait_ge(S("tap3"), 4 * c + 2 * (m // 2) + 2)
                        else:
                            dve.wait_ge(S("conv"), 12 * c + 4 * (back - 2) + m + 1)
                        y = G[:, t_ // 8, 256 * (t_ % 8) + back:256 * (t_ % 8) + 256]
                        src = ps[:, bank(J_QKV + c) + m // 2, 256 * (m % 2):256 * (m % 2) + 256 - back]
                        nc.vector.scalar_tensor_tensor(y, src, conv_col(3 - back, t_), y, ALU.mult, ALU.add)\
                            .then_inc(S("conv"), 1)
            two = lambda a: a.rearrange("p (t h) -> p t h", t=NT)
            ab = two(ps[:, 6, 256:288])
            dve.wait_ge(S("ab"), 1)
            dve.wait_ge(S("spread_in"), 80)
            nc.vector.tensor_tensor(two(g_t), ab[:, :, 0:8], dt_b.unsqueeze(1).to_broadcast([P, NT, 8]), ALU.add)\
                .then_inc(S("gate_t"), 1)
            lo_until(U_Z + 2)
            dve.wait_ge(S("qk_stat"), 16)
            mean("qk", ps[:, 7, 0:32], 32, 1.0)
            refine("qk")
            rq, rk = rms["qk"][1][:, 0:16], rms["qk"][1][:, 16:32]
            link(nc.vector.tensor_scalar(rq, rq, float(P) ** -0.5, None, ALU.mult))
            dve.wait_ge(S("gate_l"), 3)
            link(nc.vector.scalar_tensor_tensor(g_l, g_t, 0.0, g_l, ALU.max, ALU.add))
            nc.vector.scalar_tensor_tensor(two(g_g), two(g_l), -1.0, a_log_b.unsqueeze(1).to_broadcast([P, NT, 8]),
                                           ALU.mult, ALU.mult).then_inc(S("gate_g"), 1)
            link(nc.vector.tensor_scalar(g_b, g_b, 1.0, None, ALU.add))
            link(nc.vector.reciprocal(g_b, g_b))
            dve.wait_ge(S("gsum"), 1)
            link(nc.vector.tensor_copy(g_e, ps[:, 5, 0:16]))
            nc.vector.tensor_tensor(e_D, ps[:, 5, 16:32], g_e, ALU.subtract).then_inc(S("gdiff"), 1)
            lo_until(U_Z + 3)
            link(nc.vector.tensor_scalar(n_G, g_e, -1.0, None, ALU.mult))
            for n in range(16):
                dve.wait_ge(S("gb"), n // 4 + 1)
                nc.vector.scalar_tensor_tensor(G[:, 4, P * n:P * n + P], ps[:, 4 + n // 4, P * (n % 4):P * (n % 4) + P],
                                               n_G[:, tok(n):tok(n) + 1], C[:, MNEG:MNEG + P], ALU.add, ALU.add)\
                    .then_inc(S("d_arg"), 1)
            dve.wait_ge(S("gexp"), 3)
            link(nc.vector.tensor_tensor(c_a, rk, g_b, ALU.mult))
            link(nc.vector.tensor_tensor(c_kb, c_a, e_G, ALU.mult))
            nc.vector.tensor_tensor(c_kd, rk, e_D, ALU.mult).then_inc(S("gscale"), 1)
            for n in range(16):
                dve.wait_ge(S("kk"), (n | 1) + 1)
                dve.wait_ge(S("decay"), n // 4 + 1)
                nc.vector.scalar_tensor_tensor(
                    G[:, 9:11, P * n:P * n + P], ps[:, (n // 2) % 4, 256 * (n % 2):256 * (n % 2) + 256]
                    .rearrange("p (a b) -> p a b", a=2), rk[:, tok(n):tok(n) + 1],
                    G[:, 4, P * n:P * n + P].unsqueeze(1).to_broadcast([P, 2, P]), ALU.mult, ALU.mult)\
                    .then_inc(S("kk_d"), 1)
            for n in range(16):
                dve.wait_ge(S("kd"), 4 * (n // 4) + 4)
                nc.vector.tensor_scalar(G[:, 7, P * n:P * n + P], ps[:, 4 + n // 4, P * (n % 4):P * (n % 4) + P],
                                        c_kb[:, tok(n):tok(n) + 1], None, ALU.mult).then_inc(S("kbg"), 1)
            lo_until(U_Z + 4)
            quad = lambda a: a.rearrange("p (n d) -> p n d", n=4)
            over4 = lambda c: C[:, c:c + P].unsqueeze(1).to_broadcast([P, 4, P])
            Y = xn[:].rearrange("p t n -> p (t n)")
            for lv in range(LEVELS):
                for q_ in range(4):
                    a = slice(512 * q_, 512 * q_ + 512)
                    dve.wait_ge(S("t2"), 4 * lv + q_ + 1)
                    nc.vector.tensor_tensor(quad(G[:, 8, a]), quad(ps[:, q_, :]), over4(LMT + lv * P), ALU.mult)\
                        .then_inc(S("t2m"), 1)
                    if lv == 0:
                        link(nc.vector.tensor_tensor(quad(G[:, 10, a]), quad(G[:, 4, a]), over4(LM1), ALU.mult))
                        nc.vector.tensor_tensor(quad(G[:, 10, a]), over4(IDENT), quad(G[:, 10, a]), ALU.subtract)\
                            .then_inc(S("inv_x"), 1)
                        dve.wait_ge(S("t2m"), q_ + 1)
                        nc.vector.tensor_tensor(quad(Y[:, a]), over4(IDENT), quad(G[:, 8, a]), ALU.subtract)\
                            .then_inc(S("inv_y"), 1)
                for q_ in range(4 if lv else 0):
                    a = slice(512 * q_, 512 * q_ + 512)
                    dve.wait_ge(S("p12"), 4 * (lv - 1) + q_ + 1)
                    b = 4 + 2 * (q_ % 2)
                    if lv < LEVELS - 1:
                        nc.vector.tensor_tensor(G[:, 10, a], G[:, 10, a], ps[:, b, :], ALU.subtract)\
                            .then_inc(S("inv_x"), 1)
                    nc.vector.tensor_tensor(Y[:, a], Y[:, a], ps[:, b + 1, :], ALU.subtract).then_inc(S("inv_y"), 1)
            for q_ in range(4):
                dve.wait_ge(S("w_ps"), q_ + 1)
                nc.vector.tensor_copy(G[:, 8, 512 * q_:512 * q_ + 512], ps[:, 4 + q_, :]).then_inc(S("w"), 1)
            hv = lambda a: a.rearrange("p (h t d) -> p h t d", h=HEADS, t=NT)
            u4, o4 = hv(G[:, 10, :]), hv(G[:, 4, :])
            for c in range(T // CHUNK):
                tt, r = c // 2, slice(64 * (c % 2), 64 * (c % 2) + 64)
                for b in range(2 if c else 0):
                    dve.wait_ge(S("w_s"), 2 * (c - 1) + b + 1)
                    uv = u4[r, 4 * b:4 * b + 4, tt, :]
                    nc.vector.tensor_tensor(uv, uv, quad(ps[r, b, :]), ALU.subtract).then_inc(S("v_new"), 1)
                if c < 3:
                    dve.wait_ge(S("d_s"), c + 1)
                    if c == 0:
                        for b in range(2):
                            nc.vector.tensor_copy(state[:, 4 * b:4 * b + 4, :], quad(ps[:, 4 + b, :])).then_inc(S("state"), 4)
                    else:
                        for h in range(HEADS):
                            k = 16 * (c % 2) + 8 * tt + h
                            nc.vector.scalar_tensor_tensor(state[:, h, :], state[:, h, :], e_C[:, k:k + 1],
                                                           ps[:, 4 + h // 4, P * (h % 4):P * (h % 4) + P],
                                                           ALU.mult, ALU.add).then_inc(S("state"), 1)
                dve.wait_ge(S("o_ps"), c + 1)
                for b in range(2):
                    nc.vector.tensor_tensor(
                        o4[r, 4 * b:4 * b + 4, tt, :], quad(ps[r, 2 + b, :]),
                        rq[r, 8 * tt + 4 * b:8 * tt + 4 * b + 4].unsqueeze(2).to_broadcast([64, 4, P]), ALU.mult)\
                        .then_inc(S("o"), 1)
            def oT_low(b):
                dve.wait_ge(S("oT_hi"), b + 1)
                nc.vector.scalar_tensor_tensor(
                    xl[:, 2 * b:2 * b + 2, :], ps[:, 4 + b, :].rearrange("p (a t) -> p a t", a=2), gain_o(0),
                    xh[:, 2 * b:2 * b + 2, :].bitcast(F32), ALU.mult, ALU.subtract).then_inc(S("oT_lo"), 1)

            o, sq = G[:, 4, :], G[:, 7, :]
            dve.wait_ge(S("o_sq"), NT)
            n16 = lambda a: a.rearrange("p (n d) -> p n d", n=16)
            link(nc.vector.tensor_reduce(rms["og"][2], n16(sq), AX.X, ALU.add))
            mean("og", rms["og"][2], 16, P)
            refine("og")
            lo_until(U_Z + 4)
            link(nc.vector.tensor_tensor(n16(o), n16(o), rms["og"][1].unsqueeze(2).to_broadcast([P, 16, P]), ALU.mult))
            zs = G[:, 3, :].rearrange("p (t h d) -> p t h d", t=NT, h=HEADS)
            for c in range(2):
                dve.wait_ge(acc_read["A"], c + 1)
                z4 = zs[:, :, 4 * c:4 * c + 4, :].rearrange("p t h d -> p h t d")
                nc.vector.tensor_tensor(o4[:, 4 * c:4 * c + 4], o4[:, 4 * c:4 * c + 4], z4, ALU.mult)\
                    .then_inc(S("o_gated"), 1)
                if c == 0:
                    lo_until(U_AO + 1)
                    oT_low(0)
                    oT_low(1)
            oT_low(2)
            oT_low(3)
            lo_until(U_AO + 2)
            residual(U_AO, J_AO)

            def softmax(name):
                w = attn[name]
                mx, pairs = soft[name], w["heads"] // 2
                for i in range(pairs + 4):
                    if i < pairs:
                        dve.wait_ge(*past(name, "sc", i + 1))
                        if i >= 2:
                            dve.wait_ge(*past(name, "pT", i - 1))
                        b = pair_bank(i)
                        link(nc.vector.scalar_tensor_tensor(w["s"][:, i % 2], ps[:, b:b + 2, 0:3 * P], w["scale"],
                                                            w["bias"](i), ALU.mult, ALU.add))
                        for tt in range(NT):
                            nc.vector.tensor_reduce(mx[:, i % 2, 0, tt, :], w["s"][:, i % 2, :, SPAN[tt]], AX.X, ALU.max,
                                                    negate=True).then_inc(step(name, "max"), 1)
                    h = i - 1
                    if 0 <= h < pairs:
                        dve.wait_ge(*past(name, "exp", 4 * (h + 1)))
                        sums = mx[:, h % 2, 1]
                        link(nc.vector.reciprocal(sums, sums))
                        for tt in range(NT):
                            s_ = w["s"][:, h % 2, :, SPAN[tt]]
                            nc.vector.tensor_tensor(s_, s_, sums[:, tt, :].unsqueeze(2).to_broadcast([P, 2, s_.shape[2]]),
                                                    ALU.mult).then_inc(step(name, "p"), 1)
                    h = i - 3
                    if name == "b" and 0 <= h < pairs:
                        dve.wait_ge(*past("b", "pv", h + 1))
                        if h >= 2:
                            dve.wait_ge(*past("b", "out_hi", h - 1))
                        nc.vector.tensor_tensor(b_t[:, h % 2, :].rearrange("p (a t) -> p a t", a=2),
                                                pair_out("b", h)[0], b_zT[:, 2 * h:2 * h + 2], ALU.mult)\
                            .then_inc(S("b_gated"), 1)
                    h = i - 4
                    if h >= 0:
                        dve.wait_ge(*past(name, "out_hi", h + 1))
                        src, to = pair_out(name, h)
                        if name == "b":
                            src = b_t[:, h % 2, :].rearrange("p (a t) -> p a t", a=2)
                        nc.vector.tensor_tensor(xl[:, to], src, xh[:, to].bitcast(F32), ALU.subtract)\
                            .then_inc(step(name, "out"), 1)

            dve.wait_ge(S("brow_ps"), 1)
            nc.vector.tensor_copy(brow[:, 0:3 * P - 1], ps[0:HEADS, 4, 0:3 * P - 1]).then_inc(S("brow_copied"), 1)
            nc.vector.memset(brow[:, 3 * P - 1:3 * P], 0.0).then_inc(S("brow_copied"), 1)
            norm("nb", [(gain_kv, xh, xl), (gain_b, bh, bl)], U_BK + 2)
            lo_until(U_BQ + 1)
            fm_tiles = lambda t, c: t[:, 4 * c:4 * c + 4, :].rearrange("p (a m) t -> p a (m t)", a=2)
            for c in range(2):
                lo_until(U_BQ + 2 * c + 4)
                dve.wait_ge(unit_used, U_BQ + 2 * c + 2)
                nc.vector.tensor_copy(fm_tiles(b_qT, c), ps[:, bank(J_BQ + c):bank(J_BQ + c) + 2, :])\
                    .then_inc(acc_read["D"], 1)
            lo_until(U_BO + 2)
            dve.wait_ge(S("bias_w"), 8)
            softmax("b")
            residual(U_BO, J_BO)
            dve.wait_ge(*past("nfin", "ss", NT))
            mean("nfin", rms["nfin"][0], 2, D)
            refine("nfin")
            dve.wait_ge(S("gfin_in"), 16)
            for tt in range(NT):
                nc.vector.scalar_tensor_tensor(x[:, tt, :], x[:, tt, :], rms["nfin"][1][:, tt:tt + 1], gfin[:],
                                               ALU.mult, ALU.mult).then_inc(S("x_first"), 1)

            norm("nc", [(gain_c, xh, xl)], U_C + 2)
            lo_until(U_C + 3)
            dve.wait_ge(unit_used, U_C + 2)
            nc.vector.tensor_copy(c_in[:], ps[:, bank(J_C):bank(J_C) + 2, 0:416]).then_inc(acc_read["D"], 1)
            ms = rms["lat"][0]
            dve.wait_ge(S("lat_ss"), 4)
            link(nc.vector.tensor_scalar(ms[:, 0:2], ms[:, 0:2], 1.0 / 256, EPS, ALU.mult, ALU.add))
            nc.vector.tensor_scalar(ms[:, 2:4], ms[:, 2:4], 1.0 / 128, EPS, ALU.mult, ALU.add).then_inc(step("lat", "mean"), 1)
            refine("lat")
            for n, (a, b) in enumerate(((0, 256), (256, 384))):
                for tt in range(NT):
                    k = 2 * n + tt
                    nc.vector.tensor_scalar(c_n[:, tt, a:b], c_in[:, tt, a:b], rms["lat"][1][:, k:k + 1], None, ALU.mult)\
                        .then_inc(S("c_n"), 1)
            lo_until(U_SB + 3)
            for k in range(3):
                dve.wait_ge(S("lat_hi"), 2 if k < 2 else 3)
                nc.vector.scalar_tensor_tensor(cl[:, k], ps[:, 4 + k // 2, 256 * (k % 2):256 * (k % 2) + 256], gain_lat(k),
                                               ch[:, k].bitcast(F32), ALU.mult, ALU.subtract).then_inc(S("lat_lo"), 1)
            lo_until(U_LAT + 2)
            dve.wait_ge(unit_used, U_LAT + 2)
            for b in (J_LAT, J_LAT + 1):
                tt = b % 2
                nc.vector.tensor_copy(m_qk[:, tt, 0:8, :].rearrange("p h d -> p (h d)"),
                                      ps[:, 2 * tt:2 * tt + 2, :].rearrange("p b n -> p (b n)")[:, 0:768])\
                    .then_inc(acc_read["D"], 1)
            lo_until(U_SV + 2)
            dve.wait_ge(S("m_sq"), NT)
            link(nc.vector.tensor_reduce(rms["mqk"][2], m_sq[:].rearrange("p t h d -> p (t h) d"), AX.X, ALU.add))
            mean("mqk", rms["mqk"][2], 32, MLA_QK)
            refine("mqk")
            lo_until(U_CO + 1)
            ends = lambda a: a.rearrange("p n (a b) -> p n a b", b=P)[:, :, 0:3:2, :]
            over4 = lambda c: C[:, c:c + P].unsqueeze(1).unsqueeze(1).to_broadcast([P, 2, 2, P])
            for i in range(HEADS // 2 + 3):
                if i < HEADS // 2:
                    b, e_ = pair_bank(i), sb_e[:, i % 2]
                    z_ = ps[:, b:b + 2, 0:3 * P]
                    dve.wait_ge(S("sb_l"), i + 1)
                    link(nc.vector.scalar_tensor_tensor(e_, z_, 0.0, e_, ALU.max, ALU.add))
                    nc.vector.tensor_tensor(ends(e_), ends(e_), over4(STRICT), ALU.mult).then_inc(S("sb_sp"), 1)
                    dve.wait_ge(S("sb_suf"), i + 1)
                    nc.vector.tensor_tensor(ends(z_), ends(z_), over4(SBNEG), ALU.add).then_inc(S("sb_arg"), 1)
                g = i - 3
                if g >= 0:
                    dve.wait_ge(S("sb_out_hi"), g + 1)
                    nc.vector.tensor_tensor(xl[:, 4 + g], ps[:, g % 2, 0:T], xh[:, 4 + g].bitcast(F32), ALU.subtract)\
                        .then_inc(S("sb_out"), 1)
            for f in range(1, 8, 2):
                dve.wait_ge(S("m_T"), f + 1)
                nc.vector.tensor_copy(m_qkT[0:MLA_QK, 2 * f:2 * f + 2, :].rearrange("p a t -> p (a t)"),
                                      ps[0:MLA_QK, 4 + f % 4, :]).then_inc(S("m_Ts_d"), 1)
            lo_until(U_CO + 2)
            softmax("m")
            residual(U_CO, J_CO)

            def feed_forward(n, name, g_):
                norm(name, [(g_, xh, xl)], U_GU[n] + 2)
                lo_until(U_GU[n] + 2)
                b = U_GU[n]
                hTh, hTl, gs, hid = ffn[n]
                d0 = read_by("D", J_GU[n] - 1)

                def hidden(c, i=None):
                    at_ = (lambda k: k) if i is None else (lambda k: i * 2 + k)
                    dve.wait_ge(*past(f"ff{n}", "gate", at_(c + 1)))
                    nc.vector.tensor_tensor(hid[:, c % 2, :], gs[:, c % 2, :], ps[:, bank(J_GU[n] + c) + 1, :], ALU.mult)\
                        .then_inc(acc_read["D"], 1)
                    dve.wait_ge(acc_read["D"], at_(d0 + c + 1))
                    k = slice(2 * c, 2 * c + 2) if i is None else bass.ds(i * 4 + 2 * c, 2)
                    src = hid[:, c % 2, :].rearrange("p (a t) -> p a t", a=2)
                    nc.vector.tensor_copy(hTh[:, k, :], src).then_inc(step(f"ff{n}", "hi"), 1)
                    dve.wait_ge(*past(f"ff{n}", "hi", at_(c + 1)))
                    nc.vector.tensor_tensor(hTl[:, k, :], src, hTh[:, k, :].bitcast(F32), ALU.subtract)\
                        .then_inc(step(f"ff{n}", "lo"), 1)

                with dve.Fori(0, FC // 2) as i:
                    for c in range(2):
                        lo(b + 2 * c + 2, i=i)
                        lo(b + 2 * c + 3, i=i)
                        hidden(c, i)
                emitted[0] += 4 * (FC // 2)
                lo_until(b + 2 * FC + 2)
                hidden(FC - 1)
                lo_until(U_DN[n] + FT // 2 + 1)
                dve.wait_ge(unit_used, U_DN[n] + FT // 2)
                for c in range(2):
                    xs = x[:, :, 512 * c:512 * c + 512]
                    nc.vector.tensor_tensor(xs, xs, ps[:, 2 * c:2 * c + 2, :], ALU.add)\
                        .then_inc(S("final_x") if n else acc_read["D"], 1)

            feed_forward(0, "nf0", gain_f0)

            norm("nd", [(gain_d, xh, xl)], U_D + 2)
            lo_until(U_D + 2)
            ms = rms["fqk"][0].rearrange("p (t h) -> p t h", t=NT)
            for c in range(6):
                lo_until(U_D + 2 * c + 4)
                if c == 1:
                    dve.wait_ge(S("wf_hi"), 1)
                    nc.vector.tensor_tensor(wf_l[:], wf[:], wf_h[:].bitcast(F32), ALU.subtract).then_inc(S("wf_lo"), 1)
                if 1 <= c <= 4:
                    k = c - 1
                    dve.wait_ge(S("f_sq"), k + 1)
                    nc.vector.tensor_reduce(ms[:, :, 8 * k:8 * k + 8],
                                            f_sq[:, :, 512 * k:512 * k + 512].rearrange("p t (h d) -> p t h d", d=64),
                                            AX.X, ALU.add).then_inc(S("f_ssq"), 1)
                if c == 4:
                    dve.wait_ge(S("f_ssq"), 4)
                    mean("fqk", rms["fqk"][0], 64, 64)
                    dve.wait_ge(S("f_ps"), 1)
                    nc.vector.tensor_tensor(fox_t.rearrange("p (t h) -> p t h", t=NT),
                                            ps[:, 4, 0:32].rearrange("p (t h) -> p t h", t=NT),
                                            fox_b.unsqueeze(1).to_broadcast([P, NT, 16]), ALU.add).then_inc(S("f_logit"), 1)
                    refine("fqk")
                    h64 = lambda a: a.rearrange("p (h d) -> p h d", d=64)
                    nc.vector.tensor_tensor(h64(f_qk[:, 0, :]), h64(f_qk[:, 0, :]),
                                            rms["fqk"][1][:, 0:32].unsqueeze(2).to_broadcast([P, 32, 64]), ALU.mult)\
                        .then_inc(S("f_scaled0"), 1)
                    dve.wait_ge(S("f_l"), 1)
                    t16 = lambda a: a.rearrange("p (t c) -> p t c", t=NT)
                    link(nc.vector.memset(fox_w, 0.0))
                    for r in range(0, 112, 32):
                        nc.vector.scalar_tensor_tensor(fox_w[:, :, r:r + 16], t16(fox_t), 0.0, t16(fox_l), ALU.min, ALU.subtract)\
                            .then_inc(S("f_log"), 1)
            dve.wait_ge(S("f_cum"), 1)
            link(nc.vector.tensor_scalar(f_cT[:], ps[0:112, 5, 0:T], -8.0, None, ALU.mult))
            for r in (32, 96):
                nc.vector.scalar_tensor_tensor(f_cT[r:r + 16], ps[r:r + 16, 5, 0:T], -8.0, f_cT[r:r + 16].bitcast(F32),
                                               ALU.mult, ALU.subtract).then_inc(S("f_cT"), 1)
            for f in range(1, 8, 2):
                dve.wait_ge(S("f_T"), f + 1)
                nc.vector.tensor_scalar(f_qkT[:, 2 * f:2 * f + 2, :].rearrange("p a t -> p (a t)"), ps[:, 4 + f % 4, :],
                                        gain_fox(f // 4), None, ALU.mult).then_inc(S("f_Ts_d"), 1)
            lo_until(U_DO + 2)
            softmax("f")
            residual(U_DO, J_DO)
            feed_forward(1, "nf1", gain_f1)

        @block.tensor
        def _(pe):
            mm = nc.tensor.matmul

            def acc_free(j):
                if j >= 2:
                    e = readers[j - 2]
                    pe.wait_ge(acc_read[e], readers[:j - 1].count(e) * (12 if e == "C" else 1))

            def three(o_, a_h, a_l, b_h, b_l, start, stop):
                mm(o_, a_h, b_h, start=start, stop=False, skip_group_check=True)
                mm(o_, a_h, b_l, start=False, stop=False, skip_group_check=True)
                return mm(o_, a_l, b_h, start=False, stop=stop, skip_group_check=True)

            def tm(g, j, h_, l_, width=512, each=None, between=None):
                acc_free(j)
                for half in range(2):
                    if half and between:
                        between()
                    pe.wait_ge(lo_done, g + half + 1)
                    wh = whi[:, (g + half) % HIGH, 0:4 * width].rearrange("p (k n) -> p k n", k=4)
                    wl = wlo[:, (g + half) % LOW, 0:4 * width].rearrange("p (k n) -> p k n", k=4)
                    for k4 in range(4):
                        k = 4 * half + k4
                        if each:
                            pe.wait_ge(*past(each, "lo", k + 1))
                        for tt in range(NT):
                            a = slice(P * tt, P * tt + P)
                            last = three(ps[:, bank(j) + tt, 0:width], h_[:, k, a], l_[:, k, a],
                                         wh[:, k4], wl[:, k4], k == 0, k == KT - 1)
                    last.then_inc(unit_used, 1)

            def fm(g, j, h_, l_, i=None, free=True, each=None):
                if free:
                    acc_free(j)
                for half in range(2):
                    pe.wait_ge(lo_done, g + half + 1 if i is None else i * 4 + (g + half + 1))
                    wh = whi[:, (g + half) % HIGH, :].rearrange("p (k n) -> p k n", k=4)
                    wl = wlo[:, (g + half) % LOW, :].rearrange("p (k n) -> p k n", k=4)
                    for k4 in range(4):
                        k = 4 * half + k4
                        if each:
                            pe.wait_ge(*past(each, "lo", k + 1))
                        for m in range(4):
                            o_ = ps[:, bank(j) + m // 2, 256 * (m % 2):256 * (m % 2) + 256]
                            a = slice(P * m, P * m + P)
                            last = three(o_, wh[:, k4, a], wl[:, k4, a], h_[:, k], l_[:, k],
                                         k == 0 and m % 2 == 0, k == KT - 1)
                    last.then_inc(unit_used, 1)

            def turn(done, b, src):
                for n, s in enumerate(src):
                    last = nc.tensor.transpose(ps[:, b, P * n:P * n + P], s, ident)
                last.then_inc(done, 1)

            def norm(name, n_sets):
                pe.wait_ge(*past(name, "xn0", 1))
                pe.wait_ge(*past(name, "xn1", 1))
                for b in range(4):
                    turn(step(name, "T"), 4 + b, [xn[:, tt, P * k:P * k + P] for k in (2 * b, 2 * b + 1)
                                              for tt in range(NT)])

            pe.wait_ge(S("const_in"), 32)
            pe.wait_ge(S("rows_in"), 16 * 15)
            for b, n in ((0, N_ROWS0), (1, N_ROWS1)):
                nc.tensor.transpose(ps[:, 4 + b, 0:n], rows[0:n, b, :], ident[0:n, 0:n]).then_inc(S("rows_T"), 1)
            pe.wait_ge(S("cols_done"), 2)
            norm("na", 1)
            def qk_stats(c):
                pe.wait_ge(S("qk_sq"), c + 1)
                for m in range(4):
                    for tt in range(NT):
                        qk, h = (4 * c + m) // 8, (4 * c + m) % 8
                        k = 16 * qk + 8 * tt + h
                        last = mm(ps[:, 7, k:k + 1], G[:, 6 + qk, 256 * h + P * tt:256 * h + P * tt + P],
                                  C[:, ONES:ONES + 1], start=True, stop=True)
                    last.then_inc(S("qk_stat"), 1)

            for c in range(6):
                fm(U_QKV + 2 * c, J_QKV + c, xh, xl, each="na" if c == 0 else None)
                if c == 1:
                    pe.wait_ge(S("wab_lo"), 1)
                    for k in range(KT):
                        last = three(ps[0:16, 6, 0:T], wab_h[:, k], wab_l[:, k], xh[:, k], xl[:, k], k == 0, k == KT - 1)
                    last.then_inc(S("abT"), 1)
                if c == 4:
                    pe.wait_ge(S("ab_sb"), 1)
                    for tt in range(NT):
                        last = nc.tensor.transpose(ps[:, 6, 256 + 16 * tt:272 + 16 * tt], abT[:, P * tt:P * tt + P],
                                                   ident[0:16, 0:16])
                    last.then_inc(S("ab"), 1)
                if c == 1:
                    pe.wait_ge(S("masks_in"), 16)
                if c >= 2:
                    qk_stats(c - 2)
            tm(U_Z, J_Z, xh, xl)
            pe.wait_ge(S("gate_g"), 1)
            mm(ps[:, 5, 0:16], C[:, LT:LT + P], g_g, start=True, stop=True)
            mm(ps[:, 5, 16:32], C[:, BLK:BLK + P], g_g, start=True, stop=True)
            for b in range(2):
                last = mm(ps[:, 5, 32 + 16 * b:48 + 16 * b], C[:, BLK + CHUNK * b:BLK + CHUNK * b + 1].to_broadcast([P, P]),
                          g_g, start=True, stop=True)
            last.then_inc(S("gsum"), 1)
            pe.wait_ge(S("gexp"), 3)
            for q_ in range(4):
                for n in range(4 * q_, 4 * q_ + 4):
                    last = mm(ps[:, 4 + q_, P * (n % 4):P * (n % 4) + P], g_g[:, tok(n):tok(n) + 1].to_broadcast([P, P]),
                              C[:, LT:LT + P], start=True, stop=True)
                last.then_inc(S("gb"), 1)
            pe.wait_ge(S("qkv"), 6)
            pe.wait_ge(acc_read["A"], 1)
            for n in range(16):
                if n >= 8 and n % 2 == 0:
                    pe.wait_ge(S("kk_d"), n - 6)
                mm(ps[:, (n // 2) % 4, 256 * (n % 2):256 * (n % 2) + 256].rearrange("p (a b) -> p a b", a=2),
                   G[:, 1, P * n:P * n + P], G[:, 0:2, P * n:P * n + P], start=True, stop=True).then_inc(S("kk"), 1)
            for q_ in range(4):
                pe.wait_ge(S("d_arg"), 4 * q_ + 4)
                pe.wait_ge(S("d_egb"), q_ + 1)
                turn(S("k_tm"), 4 + q_, [G[:, 1, P * n:P * n + P] for n in range(4 * q_, 4 * q_ + 4)])
            for q_ in range(4):
                pe.wait_ge(S("kd"), 4 * q_ + 4)
                pe.wait_ge(S("kbg"), 4 * q_ + 4)
                turn(S("v_tm"), 4 + q_, [G[:, 2, P * n:P * n + P] for n in range(4 * q_, 4 * q_ + 4)])
            pe.wait_ge(S("kk_d"), 16)
            for q_ in range(4):
                turn(S("s_t"), q_, [G[:, 10, P * n:P * n + P] for n in range(4 * q_, 4 * q_ + 4)])
            Y = xn[:].rearrange("p t n -> p (t n)")
            for lv in range(LEVELS):
                for q_ in range(4):
                    tiles = [slice(P * n, P * n + P) for n in range(4 * q_, 4 * q_ + 4)]
                    if lv == 0:
                        pe.wait_ge(S("a_mat"), 4 * q_ + 4)
                        turn(S("t2"), q_, [G[:, 4, a] for a in tiles])
                        continue
                    pe.wait_ge(S("inv_y"), 4 * (lv - 1) + q_ + 1)
                    pe.wait_ge(S("t2m"), 4 * (lv - 1) + q_ + 1)
                    for n, a in enumerate(tiles):
                        last = mm(ps[:, q_, P * n:P * n + P], G[:, 4, a], Y[:, a], start=True, stop=True)
                    last.then_inc(S("t2"), 1)
                for q_ in range(4 if lv else 0):
                    tiles = [slice(P * n, P * n + P) for n in range(4 * q_, 4 * q_ + 4)]
                    b = 4 + 2 * (q_ % 2)
                    pe.wait_ge(S("t2m"), 4 * lv + q_ + 1)
                    pe.wait_ge(S("inv_x"), 4 * (lv - 1) + q_ + 1)
                    if q_ >= 2:
                        pe.wait_ge(S("inv_y"), 4 * lv + q_ - 1)
                    if lv == 1 and q_ == 0:
                        pe.wait_ge(S("vb"), 16)
                    for n, a in enumerate(tiles):
                        if lv < LEVELS - 1:
                            mm(ps[:, b, P * n:P * n + P], G[:, 8, a], G[:, 10, a], start=True, stop=True)
                        last = mm(ps[:, b + 1, P * n:P * n + P], G[:, 10, a], G[:, 8, a], start=True, stop=True)
                    last.then_inc(S("p12"), 1)
            for q_ in range(4):
                pe.wait_ge(S("inv_y"), 4 * (LEVELS - 1) + q_ + 1)
                for n in range(4 * q_, 4 * q_ + 4):
                    a = slice(P * n, P * n + P)
                    last = mm(ps[:, q_, P * (n % 4):P * (n % 4) + P], Y[:, a], G[:, 2, a], start=True, stop=True)
                last.then_inc(S("u_ps"), 1)
            pe.wait_ge(S("inv_y"), 4 * LEVELS)
            for q_ in range(4):
                for n in range(4 * q_, 4 * q_ + 4):
                    a = slice(P * n, P * n + P)
                    last = mm(ps[:, 4 + q_, P * (n % 4):P * (n % 4) + P], G[:, 7, a], Y[:, a], start=True, stop=True)
                last.then_inc(S("w_ps"), 1)
            pe.wait_ge(S("u"), 4)
            pe.wait_ge(S("w"), 4)
            pe.wait_ge(S("d_qdec"), 4)
            hv = lambda a: a.rearrange("p (h t d) -> p h t d", h=HEADS, t=NT)
            v4, w4, qd4, qk4, kd4 = (hv(G[:, n, :]) for n in (10, 8, 5, 9, 6))
            for c in range(T // CHUNK):
                tt, r = c // 2, slice(64 * (c % 2), 64 * (c % 2) + 64)
                part = lambda b, h: ps[r, b + h // 4, P * (h % 4):P * (h % 4) + P]
                if c:
                    for h in range(HEADS):
                        pe.wait_ge(S("state"), 8 * (c - 1) + h + 1)
                        last = mm(part(0, h), w4[:, h, tt, r], state[:, h, :], start=True, stop=True)
                        if h % 4 == 3:
                            last.then_inc(S("w_s"), 1)
                    pe.wait_ge(S("o"), 2 * c)
                for h in range(HEADS):
                    if c:
                        mm(part(2, h), qd4[:, h, tt, r], state[:, h, :], start=True, stop=False, skip_group_check=True)
                        pe.wait_ge(S("v_new"), 2 * (c - 1) + h // 4 + 1)
                    last = mm(part(2, h), qk4[r, h, tt, r], v4[r, h, tt, :], start=c == 0, stop=True,
                              skip_group_check=True)
                last.then_inc(S("o_ps"), 1)
                if c < 3:
                    for h in range(HEADS):
                        last = mm(ps[:, 4 + h // 4, P * (h % 4):P * (h % 4) + P], kd4[r, h, tt, :], v4[r, h, tt, :],
                                  start=True, stop=True)
                    last.then_inc(S("d_s"), 1)
            pe.wait_ge(S("o"), 8)
            tm(U_Z + 2, J_Z + 1, xh, xl)
            o4 = hv(G[:, 4, :])

            def turn_heads(half):
                pe.wait_ge(S("o_gated"), half + 1)
                for b in (2 * half, 2 * half + 1):
                    turn(S("oT"), 4 + b, [o4[:, h, tt, :] for h in (2 * b, 2 * b + 1) for tt in range(NT)])
                pe.wait_ge(S("oT_lo"), 2 * half + 2)

            turn_heads(0)
            tm(U_AO, J_AO, xh, xl, between=lambda: turn_heads(1))
            tm(U_AO + 2, J_AO + 1, xh, xl)

            def softmax(name):
                w = attn[name]
                pairs = w["heads"] // 2
                for i in range(pairs + 3):
                    if i < pairs:
                        if i >= 2:
                            pe.wait_ge(*past(name, "max", 2 * (i - 1)))
                        for n in range(2):
                            h = 2 * i + n
                            for tt in range(NT):
                                o_, keys = ps[:, pair_bank(i) + n, SPAN[tt]], P * (tt + 1)
                                if name == "f":
                                    r = slice(64 * n, 64 * n + 48)
                                    mm(o_, f_sel[r, h, :], f_cT[r, 0:keys], start=True, stop=False)
                                last = mm(o_, w["q"](h)[:, P * tt:P * tt + P], w["k"](h)[:, 0:keys],
                                          start=name != "f", stop=True)
                        last.then_inc(step(name, "sc"), 1)
                    h = i - 2
                    if 0 <= h < pairs:
                        pe.wait_ge(*past(name, "p", 2 * (h + 1)))
                        if h >= 1:
                            pe.wait_ge(*past(name, "pTs", h))
                        for n in range(2):
                            for b in range(3):
                                last = nc.tensor.transpose(ps[:, 6 + n, P * b:P * b + P],
                                                           w["s"][:, h % 2, n, P * b:P * b + P], ident)
                        last.then_inc(step(name, "pT"), 1)
                    h = i - 3
                    if h >= 0:
                        pe.wait_ge(*past(name, "pTs", h + 1))
                        if h >= 2:
                            pe.wait_ge(*past(name, "out", h - 1))
                            if name == "b":
                                pe.wait_ge(S("b_gated"), h - 1)
                        for n in range(2):
                            r, t0 = (slice(0, P), T * n) if name == "b" else (slice(64 * n, 64 * n + 64), 0)
                            pT, v = w["pT"][:, h % 2, n, :], w["v"]
                            mm(ps[r, h % 2, t0:t0 + T], v(2 * h + n, 0), pT[:, 0:T], start=True, stop=False,
                               skip_group_check=True)
                            last = mm(ps[r, h % 2, t0 + P:t0 + T], v(2 * h + n, 1), pT[:, T:3 * P], start=False, stop=True,
                                      skip_group_check=True)
                        last.then_inc(step(name, "pv"), 1)

            pe.wait_ge(S("relb_mask"), 1)
            pe.wait_ge(S("relb_in"), 16)
            mm(ps[0:HEADS, 4, 0:3 * P - 1], relb[:], C[0:N_BUCKETS + 1, ONEHOT:ONEHOT + 3 * P - 1],
               start=True, stop=True).then_inc(S("brow_ps"), 1)
            pe.wait_ge(S("brow_copied"), 2)
            norm("nb", 2)
            for c in range(2):
                fm(U_BK + 2 * c, J_BK + c, xh, xl, each="nb" if c == 0 else None)
            for c in range(2):
                tm(U_BV + 2 * c, J_BV + c, xh, xl)
            pe.wait_ge(S("bias_in"), 16)
            for b in range(4):
                for h in (2 * b, 2 * b + 1):
                    last = mm(ps[:, 4 + b, T * (h % 2):T * (h % 2) + T], C[:, ANTI:ANTI + P], bias_r[:, h, :],
                              start=True, stop=True)
                last.then_inc(S("bias_ps"), 1)
            pe.wait_ge(*past("nb", "lo", 2 * KT))
            for c in range(2):
                fm(U_BQ + 2 * c, J_BQ + c, bh, bl)
            for c in range(2):
                fm(U_BZ + 2 * c, J_BZ + c, bh, bl)
            pe.wait_ge(acc_read["A"], read_by("A", J_BZ + 1))
            pe.wait_ge(acc_read["D"], read_by("D", J_BQ + 1))
            pe.wait_ge(S("bias_w"), 8)
            softmax("b")
            pe.wait_ge(*past("b", "out", HEADS // 2))
            for c in range(2):
                tm(U_BO + 2 * c, J_BO + c, xh, xl)

            norm("nc", 1)
            tm(U_C, J_C, xh, xl, 416, each="nc")
            fm(U_SB, J_SB, xh, xl)
            pe.wait_ge(S("c_n"), 4)
            for b in range(2):
                turn(S("lat_T"), 4 + b, [c_n[:, tt, P * k:P * k + P] for k in ((0, 1), (2,))[b] for tt in range(NT)])
            fm(U_SB + 2, J_SB + 1, xh, xl)
            pe.wait_ge(S("lat_lo"), 3)
            pe.wait_ge(lo_done, U_LAT + 1)
            for tt in range(NT):
                for b in range(2):
                    a, c0 = slice(P * tt, P * tt + P), slice(512 * b, 512 * b + 512)
                    last = three(ps[:, 4 + 2 * tt + b, :], ch[:, 2, a], cl[:, 2, a], whi[:, U_LAT % HIGH, c0], wlo[:, U_LAT % LOW, c0], True, True)
            last.then_inc(unit_used, 1)
            acc_free(J_LAT)
            acc_free(J_LAT + 1)
            pe.wait_ge(lo_done, U_LAT + 2)
            wh, wl = (t[:, (U_LAT + 1) % n, 0:1536].rearrange("p (k n) -> p k n", k=2) for t, n in ((whi, HIGH), (wlo, LOW)))
            for tt in range(NT):
                for k in range(2):
                    for b, (c0, c1) in enumerate(((0, 512), (512, 768))):
                        a = slice(P * tt, P * tt + P)
                        last = three(ps[:, 2 * tt + b, 0:c1 - c0], ch[:, k, a], cl[:, k, a], wh[:, k, c0:c1], wl[:, k, c0:c1],
                                     k == 0, k == 1)
            last.then_inc(unit_used, 1)
            tm(U_SV, J_SV, xh, xl)
            pe.wait_ge(S("kv_read"), 2 * NT)
            pe.wait_ge(acc_read["D"], read_by("D", J_LAT + 1))
            pe.wait_ge(acc_read["A"], read_by("A", J_SV))
            for i in range(HEADS // 2 + 2):
                if i < HEADS // 2:
                    if i >= 2:
                        pe.wait_ge(S("sb_p"), i - 1)
                    for n in range(2):
                        k_, q_ = half(sbT[:, 4 + i], n), half(sbT[:, i], n)
                        z_ = ps[:, pair_bank(i) + n, :]
                        mm(z_[:, 0:T], k_[:, 0:P], q_, start=True, stop=False, skip_group_check=True)
                        last = mm(z_[:, T:3 * P], k_[:, P:T], q_[:, P:T], start=False, stop=True, skip_group_check=True)
                    last.then_inc(S("sb_z"), 1)
                g = i - 1
                if 0 <= g < HEADS // 2:
                    pe.wait_ge(S("sb_sp"), g + 1)
                    for n in range(2):
                        sp_, o_ = sb_e[:, g % 2, n, :], ps[:, pair_bank(g) + n, :]
                        mm(o_[:, 0:T], C[:, M_UPTO:M_UPTO + P], sp_[:, 0:T], start=False, stop=False, skip_group_check=True)
                        mm(o_[:, P:T], C[:, MINUS:MINUS + P], sp_[:, T:3 * P], start=False, stop=True, skip_group_check=True)
                        last = mm(o_[:, T:3 * P], C[:, M_UPTO:M_UPTO + P], sp_[:, T:3 * P], start=False, stop=True,
                                  skip_group_check=True)
                    last.then_inc(S("sb_suf"), 1)
                g = i - 2
                if g >= 0:
                    pe.wait_ge(S("sb_p"), g + 1)
                    if g >= 2:
                        pe.wait_ge(S("sb_out"), g - 1)
                    for n in range(2):
                        r, h = slice(64 * n, 64 * n + 64), 2 * g + n
                        v_, p_ = sb_v[:, :, 64 * h:64 * h + 64], sb_p[:, g % 2, n, :]
                        mm(ps[r, g % 2, 0:T], v_[:, 0], p_[:, 0:T], start=True, stop=False, skip_group_check=True)
                        last = mm(ps[r, g % 2, P:T], v_[:, 1], p_[:, T:3 * P], start=False, stop=True,
                                  skip_group_check=True)
                    last.then_inc(S("sb_pv"), 1)
            pe.wait_ge(S("rope"), 2)
            pe.wait_ge(S("sb_p"), HEADS // 2)
            for f in range(8):
                if f >= 4:
                    pe.wait_ge(S("m_Ts_a" if f % 2 == 0 else "m_Ts_d"), (f - 4) // 2 + 1)
                for n in range(4):
                    last = nc.tensor.transpose(ps[0:MLA_QK, 4 + f % 4, P * n:P * n + P], m_qk[:, n % 2, 2 * f + n // 2, :],
                                               ident)
                last.then_inc(S("m_T"), 1)
            pe.wait_ge(S("m_Ts_a"), 4)
            pe.wait_ge(S("m_Ts_d"), 4)
            pe.wait_ge(S("sb_out"), 4)
            softmax("m")
            pe.wait_ge(*past("m", "out", 4))
            for c in range(2):
                tm(U_CO + 2 * c, J_CO + c, xh, xl)

            def feed_forward(n, name):
                norm(name, 1)
                b, j = U_GU[n], J_GU[n]
                hTh, hTl, _, _ = ffn[n]
                with pe.Fori(0, FC // 2) as i:
                    for c in range(2):
                        pe.wait_ge(acc_read["D"], i * 2 + read_by("D", j + c - 2))
                        fm(b + 2 * c, j + c, xh, xl, i=i, free=False, each=name if c == 0 else None)
                fm(b + 2 * (FC - 1), j + FC - 1, xh, xl)
                b = U_DN[n]
                acc_free(J_DN[n])
                acc_free(J_DN[n] + 1)
                for u in range(FT // 2):
                    if u in (0, FT // 2 - 1):
                        pe.wait_ge(*past(f"ff{n}", "lo", FC - 1 if u == 0 else FC))
                    pe.wait_ge(lo_done, b + u + 1)
                    wh, wl = (t[:, (b + u) % n, :].rearrange("p (k n) -> p k n", k=2) for t, n in ((whi, HIGH), (wlo, LOW)))
                    for k2 in range(2):
                        k = 2 * u + k2
                        for tt in range(NT):
                            a = slice(P * tt, P * tt + P)
                            for c in range(2):
                                c0 = slice(512 * c, 512 * c + 512)
                                last = three(ps[:, 2 * c + tt, :], hTh[:, k, a], hTl[:, k, a], wh[:, k2, c0], wl[:, k2, c0],
                                             k == 0, k == FT - 1)
                    last.then_inc(unit_used, 1)

            feed_forward(0, "nf0")

            norm("nd", 1)
            for c in range(6):
                tm(U_D + 2 * c, J_D + c, xh, xl, each="nd" if c == 0 else None)
                if c == 3:
                    pe.wait_ge(S("wf_lo"), 1)
                    for tt in range(NT):
                        for k in range(KT):
                            a = slice(P * tt, P * tt + P)
                            last = three(ps[:, 4, 16 * tt:16 * tt + 16], xh[:, k, a], xl[:, k, a], wf_h[:, k], wf_l[:, k],
                                         k == 0, k == KT - 1)
                    last.then_inc(S("f_ps"), 1)
            pe.wait_ge(S("f_log"), 4)
            mm(ps[0:112, 5, 0:P], fox_w[:, 0, :], C[:, LE:LE + P], start=True, stop=True)
            mm(ps[0:112, 5, P:T], fox_w[:, 0, :], C[:, ONES:ONES + P], start=True, stop=False)
            mm(ps[0:112, 5, P:T], fox_w[:, 1, :], C[:, LE:LE + P], start=False, stop=True).then_inc(S("f_cum"), 1)
            pe.wait_ge(S("f_cT"), 2)
            pe.wait_ge(S("f_scaled0"), 1)
            pe.wait_ge(S("f_scaled1"), 1)
            for f in range(8):
                if f >= 4:
                    pe.wait_ge(S("f_Ts_a" if f % 2 == 0 else "f_Ts_d"), (f - 4) // 2 + 1)
                turn(S("f_T"), 4 + f % 4, [f_qk[:, n % 2, P * (2 * f + n // 2):P * (2 * f + n // 2) + P] for n in range(4)])
            pe.wait_ge(S("f_Ts_a"), 4)
            pe.wait_ge(S("f_Ts_d"), 4)
            pe.wait_ge(S("f_sel"), 1)
            pe.wait_ge(acc_read["A"], read_by("A", J_D + 5))
            softmax("f")
            pe.wait_ge(*past("f", "out", 8))
            for c in range(2):
                tm(U_DO + 2 * c, J_DO + c, xh, xl)
            feed_forward(1, "nf1")


_INS = ["x", "a_norm_g", "a_w_in", "a_conv_w", "a_log", "a_dt_bias", "a_out_norm_g", "a_w_out", "kv_norm_g", "w_kv",
        "b_norm_g", "b_w_in", "b_w_out", "rel_bias", "final_norm_g", "positions_2", "l0_attn_norm_2", "l0_w_in_2",
        "l0_mla_q_a_norm_2", "l0_mla_w_q_up_2", "l0_mla_kv_a_norm_2", "l0_mla_w_kv_up_2", "l0_mla_q_norm_2",
        "l0_mla_k_norm_2", "l0_w_o_2", "l0_ffn_norm_2", "l0_w_gate_2", "l0_w_up_2", "l0_w_down_2",
        "l1_attn_norm_2", "l1_w_in_2", "l1_fox_f_bias_2", "l1_fox_q_norm_2", "l1_fox_k_norm_2", "l1_w_o_2",
        "l1_ffn_norm_2", "l1_w_gate_2", "l1_w_up_2", "l1_w_down_2"]


def kernel(**inputs):
    import numpy as np
    import concourse.bacc as bacc
    from concourse.bass_utils import run_bass_kernel_spmd

    nc = bacc.Bacc("TRN2", target_bir_lowering=False, num_devices=1)
    data = {name: np.ascontiguousarray(inputs[name]) for name in _INS}
    data["consts"] = shape_constants()
    arrays, A = {}, {}
    for name, a in data.items():
        arrays[f"in_{name}"] = a
        A[name] = nc.dram_tensor(f"in_{name}", a.shape, mybir.dt.from_np(a.dtype), kind="ExternalInput").ap()
    out = nc.dram_tensor("out_0", (1, T, D), F32, kind="ExternalOutput").ap()
    block_kernel(nc, A, out)
    r = run_bass_kernel_spmd(nc, [arrays], core_ids=[0])
    return r.results[0]["out_0"]
```
